# Optimizing a Trainium2 kernel written in Bass

```python
import jax, jax.numpy as jnp
from jax import lax
import numpy as np

D_MODEL = 1024
BATCH = 1
SEQ = 512
DEPTH = 2

N_EVEN = (DEPTH + 1) // 2
N_ODD = DEPTH // 2
NORM_EPS = 1e-6

RG_WIDTH = D_MODEL
RG_HEADS = 8
RG_HEAD_DIM = RG_WIDTH // RG_HEADS
RG_CONV = 4
RG_C = 8.0
RG_CONV_LEFT = 2
SC_WIDTH = D_MODEL
SC_CONV = 3
SC_CONV_LEFT = 1
EVEN_IN = 2 * RG_WIDTH + 4 * SC_WIDTH
EVEN_MIX = RG_WIDTH + SC_WIDTH
GLA_HEADS = 4
GLA_KEY = D_MODEL // 2
GLA_VAL = D_MODEL
GLA_DK = GLA_KEY // GLA_HEADS
GLA_DV = GLA_VAL // GLA_HEADS
GLA_RANK = 16
GLA_NORMALIZER = 16.0
GLA_CHUNK = 64
ODD_IN = 2 * GLA_KEY + 2 * GLA_VAL + 2 * GLA_RANK


def rmsnorm(x, g):
    xf = x.astype(jnp.float32)
    y = xf * lax.rsqrt(jnp.mean(xf * xf, axis=-1, keepdims=True) + NORM_EPS)
    return (y * g.astype(jnp.float32)).astype(x.dtype)

def centred_dwconv(u, w, left):
    seq = u.shape[1]
    width = w.shape[0]
    up = jnp.pad(u, ((0, 0), (left, width - 1 - left), (0, 0)))
    out = up[:, 0:seq] * w[0]
    for k in range(1, width):
        out = out + up[:, k:k + seq] * w[k]
    return out

def rg_lru(u, gate_w, gate_b, lam, reverse):
    bsz, seq, width = u.shape
    uf = u.astype(jnp.float32)
    uh = uf.reshape(bsz, seq, RG_HEADS, RG_HEAD_DIM)
    gates = jax.nn.sigmoid(
        jnp.einsum('bshi,ghij->gbshj', uh, gate_w.astype(jnp.float32))
        + gate_b[:, None, None].astype(jnp.float32))
    r = gates[0].reshape(bsz, seq, width)
    i = gates[1].reshape(bsz, seq, width)
    log_a = -RG_C * r * jax.nn.softplus(-lam.astype(jnp.float32))
    a = jnp.exp(log_a)
    b = jnp.sqrt(-jnp.expm1(2.0 * log_a)) * (i * uf)

    def combine(left, right):
        a_l, b_l = left
        a_r, b_r = right
        return (a_l * a_r, a_r * b_l + b_r)

    _, h = lax.associative_scan(combine, (a, b), reverse=reverse, axis=1)
    return h

def gla_chunked(q, k, v, g):
    bsz, nh, seq, dk = q.shape
    dv = v.shape[-1]
    nc = seq // GLA_CHUNK
    qc = q.astype(jnp.float32).reshape(bsz, nh, nc, GLA_CHUNK, dk) * (dk ** -0.5)
    kc = k.astype(jnp.float32).reshape(bsz, nh, nc, GLA_CHUNK, dk)
    vc = v.astype(jnp.float32).reshape(bsz, nh, nc, GLA_CHUNK, dv)
    gc = g.reshape(bsz, nh, nc, GLA_CHUNK, dk)
    bcum = jnp.cumsum(gc, axis=3)
    btot = bcum[..., -1:, :]
    q_in = qc * jnp.exp(bcum)
    k_in = kc * jnp.exp(-bcum)
    k_st = kc * jnp.exp(btot - bcum)
    mask = jnp.tril(jnp.ones((GLA_CHUNK, GLA_CHUNK), dtype=bool))
    scores = jnp.einsum('bhnid,bhnjd->bhnij', q_in, k_in)
    scores = jnp.where(mask, scores, 0.0)
    o_intra = jnp.einsum('bhnij,bhnje->bhnie', scores, vc)
    decay = jnp.exp(btot[..., 0, :])

    def step(state, xs):
        q_n, k_n, v_n, dec_n = xs
        o_n = jnp.einsum('bhcd,bhde->bhce', q_n, state)
        state = dec_n[..., None] * state + jnp.einsum('bhcd,bhce->bhde', k_n, v_n)
        return state, o_n

    xs = (jnp.moveaxis(q_in, 2, 0), jnp.moveaxis(k_st, 2, 0),
          jnp.moveaxis(vc, 2, 0), jnp.moveaxis(decay, 2, 0))
    state0 = jnp.zeros((bsz, nh, dk, dv), jnp.float32)
    _, o_inter = lax.scan(step, state0, xs)
    o_inter = jnp.moveaxis(o_inter, 0, 2)
    return (o_intra + o_inter).reshape(bsz, nh, seq, dv)

def even_layer(x, norm_pre, norm_post, w_in, conv_w, conv_b, gate_w, gate_b, lam, sc_w, w_out):
    h = rmsnorm(x, norm_pre)
    proj = h @ w_in
    xa, za, xb, gb, gc, zb = jnp.split(
        proj, [RG_WIDTH, 2 * RG_WIDTH, 2 * RG_WIDTH + SC_WIDTH,
               2 * RG_WIDTH + 2 * SC_WIDTH, 2 * RG_WIDTH + 3 * SC_WIDTH], axis=-1)
    ua = centred_dwconv(xa, conv_w, RG_CONV_LEFT) + conv_b
    ya = rg_lru(ua, gate_w[0], gate_b[0], lam[0], False) + rg_lru(ua, gate_w[1], gate_b[1], lam[1], True)
    ya = ya * jax.nn.silu(za.astype(jnp.float32))
    yb = gb * centred_dwconv(gc * xb, sc_w, SC_CONV_LEFT)
    yb = yb * jax.nn.silu(zb)
    y = jnp.concatenate([ya, yb.astype(jnp.float32)], axis=-1) @ w_out
    return (x + rmsnorm(y, norm_post)).astype(x.dtype)

def odd_layer(x, norm_pre, norm_post, w_in, w_gate_lr, b_gate, head_norm_g, w_out):
    bsz, seq, _ = x.shape
    h = rmsnorm(x, norm_pre)
    proj = h @ w_in
    q, k, v, r, lr = jnp.split(
        proj, [GLA_KEY, 2 * GLA_KEY, 2 * GLA_KEY + GLA_VAL, 2 * GLA_KEY + 2 * GLA_VAL], axis=-1)
    lr = lr.reshape(bsz, seq, 2, GLA_RANK).astype(jnp.float32)
    z = jnp.einsum('bsdr,drk->dbsk', lr, w_gate_lr.astype(jnp.float32)) + b_gate[:, None, None].astype(jnp.float32)
    log_alpha = jax.nn.log_sigmoid(z) / GLA_NORMALIZER

    def heads(t, dh):
        return jnp.transpose(t.reshape(bsz, seq, GLA_HEADS, dh), (0, 2, 1, 3))

    qh, kh, vh = heads(q, GLA_DK), heads(k, GLA_DK), heads(v, GLA_DV)
    g_f, g_b = heads(log_alpha[0], GLA_DK), heads(log_alpha[1], GLA_DK)
    o_f = gla_chunked(qh, kh, vh, g_f)
    o_b = jnp.flip(gla_chunked(jnp.flip(qh, 2), jnp.flip(kh, 2), jnp.flip(vh, 2), jnp.flip(g_b, 2)), 2)
    o = rmsnorm(o_f + o_b, head_norm_g)
    o = jnp.transpose(o, (0, 2, 1, 3)).reshape(bsz, seq, GLA_VAL)
    y = (o * jax.nn.silu(r.astype(jnp.float32))) @ w_out
    return (x + rmsnorm(y, norm_post)).astype(x.dtype)

def first_inputs(seed: int = 0) -> dict:
    key = jax.random.key(seed)
    ks = jax.random.split(key, 20)
    nrm = jax.random.normal
    f32 = jnp.float32
    lam_a = jax.random.uniform(ks[8], (N_EVEN, 2, RG_WIDTH), f32, minval=0.9, maxval=0.999)
    lam_s = lam_a ** (1.0 / RG_C)
    rg_lambda = jnp.log(lam_s) - jnp.log1p(-lam_s)
    return {
        'x': nrm(ks[0], (BATCH, SEQ, D_MODEL), f32),
        'even_norm_pre': 1.0 + 0.05 * nrm(ks[1], (N_EVEN, D_MODEL), f32),
        'even_norm_post': 1.0 + 0.05 * nrm(ks[2], (N_EVEN, D_MODEL), f32),
        'even_w_in': nrm(ks[3], (N_EVEN, D_MODEL, EVEN_IN), f32) * D_MODEL ** -0.5,
        'rg_conv_w': nrm(ks[4], (N_EVEN, RG_CONV, RG_WIDTH), f32) * RG_CONV ** -0.5,
        'rg_conv_b': 0.01 * nrm(ks[5], (N_EVEN, RG_WIDTH), f32),
        'rg_gate_w': nrm(ks[6], (N_EVEN, 2, 2, RG_HEADS, RG_HEAD_DIM, RG_HEAD_DIM), f32) * RG_HEAD_DIM ** -0.5,
        'rg_gate_b': 0.01 * nrm(ks[7], (N_EVEN, 2, 2, RG_HEADS, RG_HEAD_DIM), f32),
        'rg_lambda': rg_lambda,
        'sc_conv_w': nrm(ks[9], (N_EVEN, SC_CONV, SC_WIDTH), f32) * SC_CONV ** -0.5,
        'even_w_out': nrm(ks[10], (N_EVEN, EVEN_MIX, D_MODEL), f32) * EVEN_MIX ** -0.5,
        'odd_norm_pre': 1.0 + 0.05 * nrm(ks[11], (N_ODD, D_MODEL), f32),
        'odd_norm_post': 1.0 + 0.05 * nrm(ks[12], (N_ODD, D_MODEL), f32),
        'odd_w_in': nrm(ks[13], (N_ODD, D_MODEL, ODD_IN), f32) * D_MODEL ** -0.5,
        'gla_w_gate_lr': nrm(ks[14], (N_ODD, 2, GLA_RANK, GLA_KEY), f32) * GLA_RANK ** -0.5,
        'gla_b_gate': 1.0 + 0.3 * nrm(ks[15], (N_ODD, 2, GLA_KEY), f32),
        'gla_norm_g': 1.0 + 0.05 * nrm(ks[16], (N_ODD, GLA_DV), f32),
        'odd_w_out': nrm(ks[17], (N_ODD, GLA_VAL, D_MODEL), f32) * GLA_VAL ** -0.5,
    }

def first_block(x, even_norm_pre, even_norm_post, even_w_in, rg_conv_w, rg_conv_b, rg_gate_w,
              rg_gate_b, rg_lambda, sc_conv_w, even_w_out, odd_norm_pre, odd_norm_post,
              odd_w_in, gla_w_gate_lr, gla_b_gate, gla_norm_g, odd_w_out):
    for layer in range(DEPTH):
        j = layer // 2
        if layer % 2 == 0:
            x = even_layer(x, even_norm_pre[j], even_norm_post[j], even_w_in[j], rg_conv_w[j],
                           rg_conv_b[j], rg_gate_w[j], rg_gate_b[j], rg_lambda[j],
                           sc_conv_w[j], even_w_out[j])
        else:
            x = odd_layer(x, odd_norm_pre[j], odd_norm_post[j], odd_w_in[j], gla_w_gate_lr[j],
                          gla_b_gate[j], gla_norm_g[j], odd_w_out[j])
    return x


N_A_LAYERS = DEPTH // 2
N_B_LAYERS = DEPTH - N_A_LAYERS
HEAD_DIM = 64
SB_HEADS = D_MODEL // HEAD_DIM
NSA_HEADS = D_MODEL // HEAD_DIM
NSA_KV_HEADS = 4
NSA_GROUP = NSA_HEADS // NSA_KV_HEADS
N_BRANCHES = 3
ROPE_DIMS = HEAD_DIM // 4
ROPE_THETA = 500000.0
D_FF = -(-8 * D_MODEL // (3 * 256)) * 256
Q_BLOCK = 128
SEL_Q_BLOCK = 64
CMP_BLOCK = 32
CMP_STRIDE = 16
CMP_HIDDEN = 4 * HEAD_DIM
SEL_BLOCK = 64
N_SEL = 8
N_LOCAL_SEL = 2
WINDOW = 512
EPS = 1e-6
NEG = -1e30
FORCE = 1e4


def _rmsnorm(x, g):
    x32 = x.astype(jnp.float32)
    y = x32 * lax.rsqrt(jnp.mean(x32 * x32, axis=-1, keepdims=True) + EPS)
    return (y * g.astype(jnp.float32)).astype(x.dtype)

def _swiglu(x, w_in, w_out):
    a, b = jnp.split(x @ w_in, 2, axis=-1)
    return (jax.nn.silu(a) * b) @ w_out

def _rope_tables(positions):
    inv_freq = jnp.power(ROPE_THETA, -jnp.arange(0, ROPE_DIMS, 2, dtype=jnp.float32) / ROPE_DIMS)
    ang = positions.astype(jnp.float32)[:, None] * inv_freq[None, :]
    return jnp.cos(ang), jnp.sin(ang)

def _apply_rope(x, cos, sin):
    half = ROPE_DIMS // 2
    x32 = x.astype(jnp.float32)
    x1, x2 = x32[..., :half], x32[..., half:ROPE_DIMS]
    c, s = cos[:, None, :], sin[:, None, :]
    return jnp.concatenate([x1 * c - x2 * s, x2 * c + x1 * s, x32[..., ROPE_DIMS:]], axis=-1).astype(x.dtype)

def _stick_breaking_attention(q, k, v):
    B, S, H, Dh = q.shape
    scale = Dh ** -0.5
    outs = []
    for start in range(0, S, Q_BLOCK):
        end = start + Q_BLOCK
        z = jnp.einsum('bthd,bshd->bhts', q[:, start:end], k[:, :end], preferred_element_type=jnp.float32) * scale
        t_pos = start + jnp.arange(Q_BLOCK)[:, None]
        s_pos = jnp.arange(end)[None, :]
        past = s_pos < t_pos
        log_1m = jnp.where(past, jax.nn.log_sigmoid(-z), 0.0)
        later = lax.cumsum(log_1m, axis=3, reverse=True) - log_1m
        w = jnp.where(past, jnp.exp(jax.nn.log_sigmoid(z) + later), 0.0)
        outs.append(jnp.einsum('bhts,bshd->bthd', w.astype(v.dtype), v[:, :end]))
    return jnp.concatenate(outs, axis=1)

def _stick_breaking_mixer(hn, w_qkv, w_out):
    B, S, _ = hn.shape
    qkv = (hn @ w_qkv).reshape(B, S, 3, SB_HEADS, HEAD_DIM)
    o = _stick_breaking_attention(qkv[:, :, 0], qkv[:, :, 1], qkv[:, :, 2])
    return o.reshape(B, S, SB_HEADS * HEAD_DIM) @ w_out

def _compress(x, pos_emb, w1, w2):
    B, S, G, Dh = x.shape
    n_cmp = (S - CMP_BLOCK) // CMP_STRIDE + 1
    idx = np.arange(n_cmp)[:, None] * CMP_STRIDE + np.arange(CMP_BLOCK)[None, :]
    blocks = x[:, idx] + pos_emb[:, None, :]
    blocks = blocks.transpose(0, 1, 3, 2, 4).reshape(B, n_cmp, G, CMP_BLOCK * Dh)
    return jax.nn.silu(blocks @ w1) @ w2

def _nsa_shared_kv(h, kv_norm, w_kv, k_norm, pos_k, pos_v, k_w1, k_w2, v_w1, v_w2, cos, sin):
    B, S, _ = h.shape
    kv = (_rmsnorm(h, kv_norm) @ w_kv).reshape(B, S, 2 * N_BRANCHES, NSA_KV_HEADS, HEAD_DIM)
    k_c_raw, v_c_raw, k_s, v_s, k_w, v_w = [kv[:, :, i] for i in range(2 * N_BRANCHES)]
    n_cmp = (S - CMP_BLOCK) // CMP_STRIDE + 1
    cc, sc = _rope_tables(jnp.arange(n_cmp) * CMP_STRIDE + (CMP_BLOCK - 1))
    k_c = _apply_rope(_rmsnorm(_compress(k_c_raw, pos_k, k_w1, k_w2), k_norm[0]), cc, sc)
    v_c = _compress(v_c_raw, pos_v, v_w1, v_w2)
    k_s = _apply_rope(_rmsnorm(k_s, k_norm[1]), cos, sin)
    k_w = _apply_rope(_rmsnorm(k_w, k_norm[2]), cos, sin)
    return (k_c, v_c, k_s, v_s, k_w, v_w)

def _nsa_selected(q, sel_idx, k_sel, v_sel):
    B, S, G, R, Dh = q.shape
    n_k = sel_idx.shape[-1]
    L = n_k * SEL_BLOCK
    scale = Dh ** -0.5
    nblk = S // SEL_Q_BLOCK
    kT = jnp.transpose(k_sel, (0, 2, 1, 3))
    vT = jnp.transpose(v_sel, (0, 2, 1, 3))
    b_ar = jnp.arange(B)[:, None, None, None]
    g_ar = jnp.arange(G)[None, :, None, None]
    offs = jnp.arange(SEL_BLOCK)
    q_blk = q.reshape(B, nblk, SEL_Q_BLOCK, G, R, Dh).transpose(1, 0, 2, 3, 4, 5)
    i_blk = sel_idx.reshape(B, G, nblk, SEL_Q_BLOCK, n_k).transpose(2, 0, 1, 3, 4)
    starts = jnp.arange(nblk) * SEL_Q_BLOCK

    def one_block(args):
        qb, ib, t0 = args
        tok = (ib[..., None] * SEL_BLOCK + offs).reshape(B, G, SEL_Q_BLOCK, L)
        kg = kT[b_ar, g_ar, tok]
        vg = vT[b_ar, g_ar, tok]
        s = jnp.einsum('btgrd,bgtld->bgrtl', qb, kg, preferred_element_type=jnp.float32) * scale
        t_pos = t0 + jnp.arange(SEL_Q_BLOCK)
        mask = tok[:, :, None] <= t_pos[:, None]
        p = jax.nn.softmax(jnp.where(mask, s, NEG), axis=-1)
        return jnp.einsum('bgrtl,bgtld->btgrd', p.astype(vg.dtype), vg)

    out = lax.map(one_block, (q_blk, i_blk, starts))
    return out.transpose(1, 0, 2, 3, 4, 5).reshape(B, S, G, R, Dh)

def _nsa_window(q, k_win, v_win):
    B, S, G, R, Dh = q.shape
    scale = Dh ** -0.5
    nblk = S // Q_BLOCK
    span = WINDOW + Q_BLOCK
    k_pad = jnp.pad(k_win, ((0, 0), (WINDOW, 0), (0, 0), (0, 0)))
    v_pad = jnp.pad(v_win, ((0, 0), (WINDOW, 0), (0, 0), (0, 0)))
    q_blk = q.reshape(B, nblk, Q_BLOCK, G, R, Dh).transpose(1, 0, 2, 3, 4, 5)
    starts = jnp.arange(nblk) * Q_BLOCK

    def one_block(args):
        qb, t0 = args
        kb = lax.dynamic_slice_in_dim(k_pad, t0, span, axis=1)
        vb = lax.dynamic_slice_in_dim(v_pad, t0, span, axis=1)
        s = jnp.einsum('btgrd,bsgd->bgrts', qb, kb, preferred_element_type=jnp.float32) * scale
        t_pos = t0 + jnp.arange(Q_BLOCK)[:, None]
        s_pos = t0 - WINDOW + jnp.arange(span)[None, :]
        mask = (s_pos <= t_pos) & (t_pos - s_pos < WINDOW) & (s_pos >= 0)
        p = jax.nn.softmax(jnp.where(mask, s, NEG), axis=-1)
        return jnp.einsum('bgrts,bsgd->btgrd', p.astype(vb.dtype), vb)

    out = lax.map(one_block, (q_blk, starts))
    return out.transpose(1, 0, 2, 3, 4, 5).reshape(B, S, G, R, Dh)

def _nsa_mixer(hn, kvs, w_in, q_norm, w_out, cos, sin):
    k_c, v_c, k_s, v_s, k_w, v_w = kvs
    B, S, _ = hn.shape
    G, R, Dh = NSA_KV_HEADS, NSA_GROUP, HEAD_DIM
    scale = Dh ** -0.5
    proj = hn @ w_in
    q = proj[..., :NSA_HEADS * Dh].reshape(B, S, NSA_HEADS, Dh)
    q = _apply_rope(_rmsnorm(q, q_norm), cos, sin).reshape(B, S, G, R, Dh)
    gates = jax.nn.sigmoid(proj[..., NSA_HEADS * Dh:].astype(jnp.float32)).reshape(B, S, N_BRANCHES, G, R)
    t_pos = jnp.arange(S)
    n_cmp = k_c.shape[1]
    s_c = jnp.einsum('btgrd,bcgd->bgrtc', q, k_c, preferred_element_type=jnp.float32) * scale
    c_end = jnp.arange(n_cmp) * CMP_STRIDE + (CMP_BLOCK - 1)
    valid_c = c_end[None, :] <= t_pos[:, None]
    p_c = jax.nn.softmax(jnp.where(valid_c, s_c, NEG), axis=-1) * jnp.any(valid_c, axis=-1)[:, None]
    o_c = jnp.einsum('bgrtc,bcgd->btgrd', p_c.astype(v_c.dtype), v_c)
    n_sel = S // SEL_BLOCK
    c_start = np.arange(n_cmp) * CMP_STRIDE
    j_start = np.arange(n_sel) * SEL_BLOCK
    overlap = ((c_start[:, None] < j_start[None, :] + SEL_BLOCK)
               & (c_start[:, None] + CMP_BLOCK > j_start[None, :])).astype(np.float32)
    imp = jnp.einsum('bgrtc,cj->bgtj', p_c, jnp.asarray(overlap))
    j = jnp.arange(n_sel)[None, :]
    cur = (t_pos // SEL_BLOCK)[:, None]
    forced = (j == 0) | ((cur - j >= 0) & (cur - j < N_LOCAL_SEL))
    sel_score = jnp.where(forced, FORCE, jnp.where(j <= cur, imp, -FORCE))
    _, sel_idx = lax.top_k(sel_score, min(N_SEL, n_sel))
    o_s = _nsa_selected(q, sel_idx, k_s, v_s)
    o_w = _nsa_window(q, k_w, v_w)
    o = (gates[:, :, 0, :, :, None] * o_c + gates[:, :, 1, :, :, None] * o_s
         + gates[:, :, 2, :, :, None] * o_w).astype(hn.dtype)
    return o.reshape(B, S, NSA_HEADS * Dh) @ w_out

def second_inputs(seed: int = 0) -> dict:
    key = jax.random.key(seed)
    ks = jax.random.split(key, 22)
    f32 = jnp.float32

    def dense(k, shape):
        return jax.random.normal(k, shape, f32) * shape[-2] ** -0.5

    def gain(k, shape):
        return 1.0 + 0.02 * jax.random.normal(k, shape, f32)

    H, G, Dh = NSA_HEADS, NSA_KV_HEADS, HEAD_DIM
    return {
        'x': jax.random.normal(ks[0], (BATCH, SEQ, D_MODEL), f32),
        'ffn1_norm': gain(ks[1], (DEPTH, D_MODEL)),
        'ffn1_w_in': dense(ks[2], (DEPTH, D_MODEL, 2 * D_FF)),
        'ffn1_w_out': dense(ks[3], (DEPTH, D_FF, D_MODEL)),
        'mix_norm': gain(ks[4], (DEPTH, D_MODEL)),
        'ffn2_norm': gain(ks[5], (DEPTH, D_MODEL)),
        'ffn2_w_in': dense(ks[6], (DEPTH, D_MODEL, 2 * D_FF)),
        'ffn2_w_out': dense(ks[7], (DEPTH, D_FF, D_MODEL)),
        'sb_w_qkv': dense(ks[8], (N_A_LAYERS, D_MODEL, 3 * SB_HEADS * Dh)),
        'sb_w_out': dense(ks[9], (N_A_LAYERS, SB_HEADS * Dh, D_MODEL)),
        'kv_norm': gain(ks[10], (D_MODEL,)),
        'nsa_w_kv': dense(ks[11], (D_MODEL, 2 * N_BRANCHES * G * Dh)),
        'nsa_k_norm': gain(ks[12], (N_BRANCHES, Dh)),
        'cmp_pos_k': 0.1 * jax.random.normal(ks[13], (CMP_BLOCK, Dh), f32),
        'cmp_pos_v': 0.1 * jax.random.normal(ks[14], (CMP_BLOCK, Dh), f32),
        'cmp_k_w1': dense(ks[15], (CMP_BLOCK * Dh, CMP_HIDDEN)),
        'cmp_k_w2': dense(ks[16], (CMP_HIDDEN, Dh)),
        'cmp_v_w1': dense(ks[17], (CMP_BLOCK * Dh, CMP_HIDDEN)),
        'cmp_v_w2': dense(ks[18], (CMP_HIDDEN, Dh)),
        'nsa_w_in': dense(ks[19], (N_B_LAYERS, D_MODEL, H * Dh + N_BRANCHES * H)),
        'nsa_q_norm': gain(ks[20], (N_B_LAYERS, Dh)),
        'nsa_w_out': dense(ks[21], (N_B_LAYERS, H * Dh, D_MODEL)),
    }

def second_block(x, ffn1_norm, ffn1_w_in, ffn1_w_out, mix_norm, ffn2_norm, ffn2_w_in, ffn2_w_out,
              sb_w_qkv, sb_w_out, kv_norm, nsa_w_kv, nsa_k_norm, cmp_pos_k, cmp_pos_v,
              cmp_k_w1, cmp_k_w2, cmp_v_w1, cmp_v_w2, nsa_w_in, nsa_q_norm, nsa_w_out):
    B, S, _ = x.shape
    cos, sin = _rope_tables(jnp.arange(S))
    h = x
    kvs = None
    for layer in range(DEPTH):
        h = h + 0.5 * _swiglu(_rmsnorm(h, ffn1_norm[layer]), ffn1_w_in[layer], ffn1_w_out[layer])
        hn = _rmsnorm(h, mix_norm[layer])
        if layer < N_A_LAYERS:
            h = h + _stick_breaking_mixer(hn, sb_w_qkv[layer], sb_w_out[layer])
        else:
            i = layer - N_A_LAYERS
            h = h + _nsa_mixer(hn, kvs, nsa_w_in[i], nsa_q_norm[i], nsa_w_out[i], cos, sin)
        h = h + 0.5 * _swiglu(_rmsnorm(h, ffn2_norm[layer]), ffn2_w_in[layer], ffn2_w_out[layer])
        if layer == N_A_LAYERS - 1:
            kvs = _nsa_shared_kv(h, kv_norm, nsa_w_kv, nsa_k_norm, cmp_pos_k, cmp_pos_v,
                                 cmp_k_w1, cmp_k_w2, cmp_v_w1, cmp_v_w2, cos, sin)
    return h


def setup_inputs(seed=0):
    out = dict(first_inputs(seed))
    for name, value in second_inputs(seed + 1).items():
        if name != "x":
            out[name + "_2"] = value
    return out


def reference(
    x, even_norm_pre, even_norm_post, even_w_in, rg_conv_w, rg_conv_b, rg_gate_w, rg_gate_b,
    rg_lambda, sc_conv_w, even_w_out, odd_norm_pre, odd_norm_post, odd_w_in, gla_w_gate_lr,
    gla_b_gate, gla_norm_g, odd_w_out, ffn1_norm_2, ffn1_w_in_2, ffn1_w_out_2, mix_norm_2,
    ffn2_norm_2, ffn2_w_in_2, ffn2_w_out_2, sb_w_qkv_2, sb_w_out_2, kv_norm_2, nsa_w_kv_2,
    nsa_k_norm_2, cmp_pos_k_2, cmp_pos_v_2, cmp_k_w1_2, cmp_k_w2_2, cmp_v_w1_2, cmp_v_w2_2,
    nsa_w_in_2, nsa_q_norm_2, nsa_w_out_2,
):
    x = first_block(
        x, even_norm_pre, even_norm_post, even_w_in, rg_conv_w, rg_conv_b, rg_gate_w, rg_gate_b,
        rg_lambda, sc_conv_w, even_w_out, odd_norm_pre, odd_norm_post, odd_w_in, gla_w_gate_lr,
        gla_b_gate, gla_norm_g, odd_w_out,
    )
    return second_block(
        x, ffn1_norm_2, ffn1_w_in_2, ffn1_w_out_2, mix_norm_2, ffn2_norm_2, ffn2_w_in_2,
        ffn2_w_out_2, sb_w_qkv_2, sb_w_out_2, kv_norm_2, nsa_w_kv_2, nsa_k_norm_2, cmp_pos_k_2,
        cmp_pos_v_2, cmp_k_w1_2, cmp_k_w2_2, cmp_v_w1_2, cmp_v_w2_2, nsa_w_in_2, nsa_q_norm_2,
        nsa_w_out_2,
    )


_drawn_inputs = setup_inputs


def setup_inputs(seed=0):
    import zlib

    import numpy as np

    out = dict(_drawn_inputs(seed))
    spreads = {}
    factors = {'rg_gate_b': 8.0,
     'ffn1_norm_2': 8.0,
     'mix_norm_2': 6.218,
     'ffn2_norm_2': 8.0,
     'kv_norm_2': 8.0,
     'nsa_k_norm_2': 8.0,
     'cmp_pos_k_2': 8.0,
     'cmp_pos_v_2': 36.208,
     'nsa_q_norm_2': 8.0}
    for name, (base, spread) in spreads.items():
        noise = np.random.default_rng([zlib.crc32(name.encode()), seed]).standard_normal(out[name].shape)
        drawn = base * np.exp(spread * noise) if base else spread * noise
        out[name] = __import__('jax').numpy.asarray(drawn.astype(out[name].dtype))
    for name, factor in factors.items():
        out[name] = (out[name] * factor).astype(out[name].dtype)
    return out
```

```python
from contextlib import ExitStack

import numpy as np
import concourse.bass as bass
from concourse import mybir

F32 = mybir.dt.float32
U32 = mybir.dt.uint32
ACT = mybir.ActivationFunctionType
ALU = mybir.AluOpType
AX = mybir.AxisListType.X

P = 128
D = 1024
T = 512
DT = D // P
TT = T // P
EPS = 1e-6
RG_HEADS = 8
GLA_HEADS, GLA_DK, GLA_DV, GLA_RANK, GLA_CHUNK = 4, 128, 256, 16, 64
GLA_NCH = T // GLA_CHUNK
D_FF = 2816
FT = D_FF // P
HD = 64
SB_PAIRS = D // (2 * HD)
KV_HEADS = 4
N_CMP = (T - 32) // 16 + 1
NEG = -1e30
RING = 4
SLOT = 11 * P
LOG_SET = "natural_log_exp_and_others"

STREAM = [
    ("even_in", 48, 8 * P), ("even_out", 16, 8 * P),
    ("odd_qkr", 16, 8 * P), ("odd_v", 8, 8 * P), ("odd_out", 8, 8 * P),
    ("ffn1_in_0", 44, 8 * P), ("ffn1_out_0", 16, 11 * P),
    ("sb_qk", 16, 8 * P), ("sb_v", 8, 8 * P), ("sb_out", 8, 8 * P),
    ("ffn2_in_0", 44, 8 * P), ("ffn2_out_0", 16, 11 * P),
    ("kv_t", 8, 8 * P), ("kv_v", 4, 8 * P), ("cmp_w1", 8, 8 * P),
    ("ffn1_in_1", 44, 8 * P), ("ffn1_out_1", 16, 11 * P),
    ("nsa_q", 8, 8 * P), ("nsa_out", 8, 8 * P),
    ("ffn2_in_1", 44, 8 * P), ("ffn2_out_1", 16, 11 * P),
]

CONSTS = [
    ("g_even_pre", 8), ("g_even_post", 8), ("g_odd_pre", 8), ("g_odd_post", 8),
    ("g_ffn1_0", 8), ("g_ffn1_1", 8), ("g_mix_0", 8), ("g_mix_1", 8), ("g_ffn2_0", 8), ("g_ffn2_1", 8),
    ("g_kv", 8), ("lam", 16), ("gla_bias", 8), ("gla_g", 2), ("q_norm", 1), ("k_norm", 3),
    ("pos_k", 16), ("pos_v", 16), ("eps", 1), ("valid", 4),
    ("w_lr", 256), ("w_gate_lr", 1024), ("w2_k", 128), ("w2_v", 128), ("w_gates", 384),
    ("ident", 128), ("ones", 128), ("halves", 128), ("rot", 128), ("neg_tri", 128), ("neg_ones", 128),
    ("sb_neg", 128), ("sb_keep", 128), ("causal_neg", 128), ("gla_keep", 1024), ("chunk_keep", 1024),
    ("cos", 512), ("sin", 512), ("cos_c", 124), ("sin_c", 124), ("neg_c", 124),
]
CONST_AT = {}
_at = 0
for _name, _n in CONSTS:
    CONST_AT[_name] = (_at, _n)
    _at += _n
N_CONSTS = _at
GATE_COLS = 4 * P + 16

SIGNALS = """
x_landed const_landed out_stored phase_end slots_used
squares_ready sumsq_ready root_ready
even_copied ua_ready gates_done gates_read decay_ready factor_ready root_b_ready even_channel_done
even_out_copied proj_copied v_copied lr_done lr_copied res_added
gate_inputs gate_done gate_log cum_ready exps_ready qk_scaled scores_done scores_masked kst_copied
updates_done states_ready o_done o_squared o_scaled o_turned o_stored
silu_done hidden_ready down_done
sb_copies z_done log_done sp_ready later_done w_done pv_done sb_stored
hr_squares hr_sums hr_root hr_normed hr_rotated
xb_ready cmp_silu cmp_out cmp_copied gates_mm
q_static z2_done max_ready probs_ready turned turned_copied attended combined mix_turned mix_copied
""".split()


def build(nc, x_in, consts_in, gates_in, weights, out):
    ctx = ExitStack()
    with ctx:
        sem = {}
        for name in SIGNALS:
            sem[name] = ctx.enter_context(nc.semaphore(name))
        landed = [ctx.enter_context(nc.semaphore(f"slot_landed_{j}")) for j in range(RING)]
        gate_landed = [ctx.enter_context(nc.semaphore(f"gate_landed_{j}")) for j in range(2)]

        def sb(name, cols):
            return ctx.enter_context(nc.sbuf_tensor(name, [P, cols], F32))

        res = sb("res", DT * T)[:, :].rearrange("p (k t) -> p k t", t=T)
        hn = sb("hn", DT * T)[:, :].rearrange("p (k t) -> p k t", t=T)
        hn_flat = hn.rearrange("p k t -> p (k t)")
        res_flat = res.rearrange("p k t -> p (k t)")
        ring = sb("ring", RING * SLOT)[:, :].rearrange("p (j c) -> p j c", j=RING)
        consts = sb("consts", N_CONSTS)
        root = sb("root", T)
        rinv = sb("rinv", T)
        ARENA = 31400
        arena = sb("arena", ARENA)
        ps = ctx.enter_context(nc.psum_tensor("ps", [P, 8, 512], F32))

        def con(name):
            at, n = CONST_AT[name]
            return consts[:, at:at + n]

        ident, ones = con("ident"), con("ones")
        eps = con("eps")

        class Region:
            def __init__(self, start=0):
                self.at = start

            def take(self, cols):
                a = self.at
                self.at += cols
                assert self.at <= ARENA, self.at
                return arena[:, a:a + cols]

            def tiles(self, k, n=T):
                return self.take(k * n).rearrange("p (k t) -> p k t", t=n)

        first = {}
        n0 = 0
        for name, slots, cols in STREAM:
            first[name] = n0
            n0 += slots
        slots_of = {name: slots for name, slots, _ in STREAM}

        def used(name, n):
            return n + (first[name] + RING)

        phase = {"n": {}}
        phase_total = 34

        def barrier(eng, who):
            n = phase["n"].get(who, 0) + 1
            phase["n"][who] = n
            eng.drain().then_inc(sem["phase_end"], 1)
            eng.wait_ge(sem["phase_end"], 4 * n)

        def update_of(d, n):
            bank = ([0, 1, 6, 7] if d == 0 else [2, 3, 4, 5])[n // 4 * 2 + n % 2]
            return ps[:, bank, n // 2 % 2 * GLA_DV:(n // 2 % 2 + 1) * GLA_DV]

        def wait_alone(eng, name, value):
            eng.wait_ge(sem["const_landed"], 16)
            eng.wait_ge(sem[name], value)

        norms = {"act": 0, "pe": 0, "dve": 0}

        def norm_act(act, src_flat, sq_flat):
            n = norms["act"]
            norms["act"] += 1
            for half in range(2):
                cols = slice(half * 4 * T, (half + 1) * 4 * T)
                nc.scalar.activation(sq_flat[:, cols], src_flat[:, cols], ACT.Square).then_inc(sem["squares_ready"], 1)
            act.wait_ge(sem["sumsq_ready"], n + 1)
            nc.scalar.activation(root[:, :], ps[:, 7, :], ACT.Sqrt, bias=eps, scale=1.0 / D).then_inc(sem["root_ready"], 1)

        def norm_pe(pe, sq):
            n = norms["pe"]
            norms["pe"] += 1
            for k in range(DT):
                if k % 4 == 0:
                    pe.wait_ge(sem["squares_ready"], 2 * n + k // 4 + 1)
                last = nc.tensor.matmul(ps[:, 7, :], ones, sq[:, k, :], start=(k == 0), stop=(k == DT - 1))
            last.then_inc(sem["sumsq_ready"], 1)

        def norm_dve(dve, src, gain, dst):
            n = norms["dve"]
            norms["dve"] += 1
            dve.wait_ge(sem["root_ready"], n + 1)
            nc.vector.reciprocal(rinv[:, :], root[:, :])
            dve.drain()
            for k in range(DT):
                nc.vector.scalar_tensor_tensor(dst[:, k, :], src[:, k, :], con(gain)[:, k:k + 1], rinv[:, :],
                                               ALU.mult, ALU.mult)

        def project_pe(pe, name, x, free, per_tile=1):
            kt = (SLOT if "out_" in name else 8 * P) // P
            with pe.Fori(0, slots_of[name] // RING) as i:
                for j in range(RING):
                    t, part = j // per_tile, j % per_tile
                    if part == 0:
                        pe.wait_ge(sem[free[0]], (RING // per_tile) * i + (free[1] + t + 1))
                    pe.wait_ge(landed[j], 16 * i + 16 * (first[name] // RING + 1))
                    for k in range(kt):
                        mm = nc.tensor.matmul(ps[:, t, :], ring[:, j, k * P:(k + 1) * P], x[:, part * kt + k, :],
                                              start=(part == 0 and k == 0), stop=(part == per_tile - 1 and k == kt - 1))
                    mm.then_inc(sem["slots_used"], 1)

        def copy_out_act(act, name, free, dst, per_tile=1, func=ACT.Copy, scale=1.0, tiles=None, at=0):
            banks = RING // per_tile
            with act.Fori(0, slots_of[name] // RING) as i:
                for t in range(banks):
                    act.wait_ge(sem["slots_used"], used(name, RING * i + per_tile * (t + 1)))
                    nc.scalar.activation(dst[:, banks * i + t, :], ps[:, t, :], func, scale=scale)\
                        .then_inc(sem[free[0]], 1)

        def project_v_pe(pe, name, copied):
            groups = slots_of[name] // RING
            for g in range(groups):
                if g > 0:
                    pe.wait_ge(sem["v_copied"], copied + TT * g)
                for j in range(RING):
                    pe.wait_ge(landed[j], 16 * (first[name] // RING + 1 + g))
                    for k2 in range(2):
                        k = 2 * j + k2
                        for t in range(TT):
                            mm = nc.tensor.matmul(ps[:, 4 + t, :], hn[:, k, t * P:(t + 1) * P],
                                                  ring[:, j, k2 * 512:(k2 + 1) * 512],
                                                  start=(k == 0), stop=(k == DT - 1))
                    mm.then_inc(sem["slots_used"], 1)

        def copy_v_act(act, name, dst):
            for g in range(slots_of[name] // RING):
                act.wait_ge(sem["slots_used"], used(name, RING * (g + 1)))
                for t in range(TT):
                    nc.scalar.activation(dst[:, t, g * 512:(g + 1) * 512], ps[:, 4 + t, :], ACT.Copy)\
                        .then_inc(sem["v_copied"], 1)

        r = Region()
        y_even = r.tiles(16)
        ytmp = r.tiles(DT)
        ytmp_flat = ytmp.rearrange("p k t -> p (k t)")
        r = Region(16 * T)
        gw = r.tiles(2, GATE_COLS)
        xa_pad, xb_s, gc_s, gb_s, szb, sza, ua = (r.tiles(2, n) for n in (516, T, T, T, T, T, T))
        u_pad, cv = r.take(516), r.take(T)
        rg, ig, ag, tg, hg = (r.tiles(2) for _ in range(5))
        sg = tg
        nsp = r.take(16)
        nsp_c = r.tiles(2, 2)
        lt = r.tiles(6, 16)

        r = Region()
        qk_o = r.tiles(8)
        r_o = r.tiles(8)
        v_o = r.tiles(TT, GLA_HEADS * GLA_DV)
        lr_t = r.take(T)
        wz = r.tiles(2, P)
        bz = r.take(2)
        vh = r.tiles(TT, GLA_DV)
        bc, e_p, e_n, q_in, k_in, k_st, kstn, st = (r.tiles(2) for _ in range(8))
        states = r.take(2 * GLA_NCH * GLA_DV).rearrange("p (d n e) -> p d n e", d=2, e=GLA_DV)
        e_t, zb_o, la_o = states[:, :, 0:2, :].rearrange("p d n e -> p d (n e)"), q_in, k_in
        on_o = r.tiles(TT, GLA_DV)
        ssum, sroot, sinv = r.take(TT), r.take(TT), r.take(TT)
        ytmp_o, ytmp_o_flat = qk_o, qk_o.rearrange("p k t -> p (k t)")
        odd_end = r.at

        r = Region()
        k_sw = r.tiles(8)
        v_sw = r.tiles(TT, 512)
        k_c = r.take(KV_HEADS * N_CMP)
        v_c = r.take(KV_HEADS * HD)
        KEPT = r.at

        r = Region(KEPT)
        hid = r.tiles(FT)
        silu_a = r.tiles(2)

        r = Region()
        qk_s = r.tiles(16)
        v_s = r.tiles(TT, D)
        CUT = [0, 512, 896, 1152, 1280]
        q_st, k_st_s = r.tiles(2), r.tiles(2)
        v_st = r.take(2 * TT * P).rearrange("p (b k d) -> p b k d", b=2, d=P)
        lg, sp_b, wb = r.tiles(2, 1280), r.tiles(2, 1280), r.tiles(2, 1280)

        r = Region(KEPT)
        kt8 = r.tiles(8)
        hr_sq, hr_xn, hr_t1, hr_t2 = (r.take(T) for _ in range(4))
        x2 = r.take(2 * 4 * T).rearrange("p (c g t) -> p c g t", c=2, t=T)
        xb = r.take(2 * 16 * 124).rearrange("p (c m n) -> p c m n", c=2, n=124)
        hid_c = r.take(4 * 124).rearrange("p (c m n) -> p c m n", c=2, n=124)
        kc_raw = r.take(124)

        r = Region(KEPT)
        q_h = r.tiles(16)
        o_n = r.tiles(TT, D)
        q_t = r.tiles(8)
        hr2_sq, hr2_xn, hr2_t1, hr2_t2 = (r.take(T) for _ in range(4))
        r = Region(KEPT + 16 * T + TT * D)
        pr, prt = r.tiles(2, 1280), r.tiles(2, 1280)
        q_s2 = r.tiles(2)
        zmax, psm, coef = r.tiles(2, 4), r.tiles(2, 4), r.tiles(2, 4)
        gts = r.tiles(TT, 48)
        k_c3 = k_c.rearrange("p (g n) -> p g n", n=N_CMP)
        v_c3 = v_c.rearrange("p (g d) -> p g d", d=HD)
        v_sw4 = v_sw.rearrange("p t (b d) -> p t b d", d=HD)
        o_n4 = o_n.rearrange("p t (h d) -> p t h d", d=HD)
        gts_g = gts.rearrange("p t g -> p g t")

        block = ctx.enter_context(nc.Block())

        @block.sync
        def _(sp):
            sp.dma_start(consts[:, :], consts_in).then_inc(sem["const_landed"], 16)
            sp.dma_start(res[:, :, :], x_in).then_inc(sem["x_landed"], 16)
            for name, slots, cols in STREAM:
                if name == "even_in":
                    with sp.Fori(0, RG_HEADS // 2) as i:
                        for jj in range(2):
                            sp.wait_ge(sem["even_channel_done"], 2 * i + (jj + 1))
                            sp.dma_start(gw[:, jj, :], gates_in[2 * i + jj]).then_inc(gate_landed[jj], 16)
                            for n in range(6):
                                s = 6 * jj + n
                                sp.wait_ge(sem["slots_used"], 12 * i + (s + 1))
                                sp.dma_start(ring[:, s % RING, 0:cols], weights[name][12 * i + s])\
                                    .then_inc(landed[s % RING], 16)
                    continue
                with sp.Fori(0, slots // RING) as i:
                    for j in range(RING):
                        sp.wait_ge(sem["slots_used"], RING * i + (first[name] + j + 1))
                        sp.dma_start(ring[:, j, 0:cols], weights[name][RING * i + j]).then_inc(landed[j], 16)
            sp.wait_ge(sem["phase_end"], 4 * phase_total)
            sp.dma_start(out, res[:, :, :]).then_inc(sem["out_stored"], 16)
            sp.wait_ge(sem["out_stored"], 16)

        @block.tensor
        def _(pe):
            B = lambda: barrier(pe, "pe")
            pe.sem_inc(sem["slots_used"], RING)
            pe.wait_ge(sem["const_landed"], 16)

            norm_pe(pe, hn)
            B()
            with pe.Fori(0, RG_HEADS // 2) as i:
                for jj in range(2):
                    for n in range(6):
                        s = 6 * jj + n
                        j = s % RING
                        pe.wait_ge(sem["even_copied"], 12 * i + (s + 1))
                        pe.wait_ge(landed[j], 48 * i + 16 * (s // RING + 1))
                        for k in range(DT):
                            mm = nc.tensor.matmul(ps[:, j, :], ring[:, j, k * P:(k + 1) * P], hn[:, k, :],
                                                  start=(k == 0), stop=(k == DT - 1))
                        mm.then_inc(sem["slots_used"], 1)
                    pe.wait_ge(sem["ua_ready"], 2 * i + (jj + 1))
                    pe.wait_ge(sem["gates_read"], 2 * i + (jj + 1))
                    pe.wait_ge(gate_landed[jj], 16 * i + 16)
                    for g in range(4):
                        mm = nc.tensor.matmul(ps[:, 4 + g, :], gw[:, jj, g * P:(g + 1) * P], ua[:, jj, :],
                                              start=True, stop=True)
                    mm.then_inc(sem["gates_done"], 1)
            B()
            project_pe(pe, "even_out", y_even, ("even_out_copied", 0), per_tile=2)
            B()
            norm_pe(pe, hn)
            B()

            norm_pe(pe, hn)
            B()
            project_pe(pe, "odd_qkr", hn, ("proj_copied", 0))
            for k in range(DT):
                mm = nc.tensor.matmul(ps[0:32, 7, :], con("w_lr")[:, k * 32:(k + 1) * 32], hn[:, k, :],
                                      start=(k == 0), stop=(k == DT - 1))
            mm.then_inc(sem["lr_done"], 1)
            pe.wait_ge(sem["lr_copied"], 1)
            project_v_pe(pe, "odd_v", 0)
            B()
            with pe.Fori(0, GLA_HEADS) as h:
                pe.wait_ge(sem["gate_inputs"], h + 1)
                for d in range(2):
                    mm = nc.tensor.matmul(ps[:, d, :], wz[0:32, d, :], lr_t[0:32, :], start=True, stop=True)
                mm.then_inc(sem["gate_done"], 1)
                pe.wait_ge(sem["qk_scaled"], h + 1)
                for d in range(2):
                    for t in range(TT):
                        c = slice(t * P, (t + 1) * P)
                        nc.tensor.matmul(ps[:, 2 + d, c], k_in[:, d, c], q_in[:, d, c], start=True, stop=True)
                        mm = nc.tensor.transpose(ps[:, 4 + d, c], k_st[:, d, c], ident)
                mm.then_inc(sem["scores_done"], 1)
                pe.wait_ge(sem["kst_copied"], h + 1)
                pe.wait_ge(sem["scores_masked"], h + 1)
                for d in range(2):
                    for n in range(GLA_NCH):
                        if n == (GLA_NCH - 1 if d == 0 else 0):
                            continue
                        lo = GLA_CHUNK * (n % 2)
                        rows = slice(lo, lo + GLA_CHUNK)
                        mm = nc.tensor.matmul(update_of(d, n),
                                              kstn[rows, d, (n // 2) * P:(n // 2 + 1) * P], vh[rows, n // 2, :],
                                              start=True, stop=True)
                mm.then_inc(sem["updates_done"], 1)
                pe.wait_ge(sem["states_ready"], h + 1)
                for t in range(TT):
                    c = slice(t * P, (t + 1) * P)
                    for d in range(2):
                        nc.tensor.matmul(ps[:, t, 0:GLA_DV], st[:, d, c], vh[:, t, :], start=(d == 0), stop=False,
                                         skip_group_check=True)
                    for half in range(2):
                        n = 2 * t + half
                        for d in range(2):
                            if n == (0 if d == 0 else GLA_NCH - 1):
                                continue
                            mm = nc.tensor.matmul(ps[GLA_CHUNK * half:GLA_CHUNK * (half + 1), t, 0:GLA_DV],
                                                  q_in[:, d, n * GLA_CHUNK:(n + 1) * GLA_CHUNK], states[:, d, n, :],
                                                  start=False, stop=True, skip_group_check=True)
                mm.then_inc(sem["o_done"], 1)
                pe.wait_ge(sem["o_scaled"], h + 1)
                for e in range(2):
                    for t in range(TT):
                        mm = nc.tensor.transpose(ps[:, 4 + e, t * P:(t + 1) * P], on_o[:, t, e * P:(e + 1) * P], ident)
                mm.then_inc(sem["o_turned"], 1)
            B()
            project_pe(pe, "odd_out", hn, ("proj_copied", 16))
            B()
            norm_pe(pe, hn)
            B()

            def ffn_pe(which, layer, nth):
                norm_pe(pe, hn)
                B()
                name = f"{which}_in_{layer}"
                with pe.Fori(0, slots_of[name] // RING) as i:
                    for j in range(RING):
                        if j % 2 == 0:
                            pe.wait_ge(sem["hidden_ready"], 2 * i + (FT * nth + j // 2 + 1))
                        pe.wait_ge(landed[j], 16 * i + 16 * (first[name] // RING + 1))
                        for k in range(DT):
                            mm = nc.tensor.matmul(ps[:, j, :], ring[:, j, k * P:(k + 1) * P], hn[:, k, :],
                                                  start=(k == 0), stop=(k == DT - 1))
                        mm.then_inc(sem["slots_used"], 1)
                B()
                project_pe(pe, f"{which}_out_{layer}", hid, ("down_done", 8 * nth), per_tile=2)
                B()

            ffn_pe("ffn1", 0, 0)

            norm_pe(pe, hn)
            B()
            project_pe(pe, "sb_qk", hn, ("proj_copied", 24))
            project_v_pe(pe, "sb_v", 8)
            B()
            with pe.Fori(0, SB_PAIRS // 2) as i:
                def z_mm(u):
                    pair, e = u // 2, u % 2
                    rows = slice(64 * e, 64 * e + 64)
                    pe.wait_ge(sem["sb_copies"], 2 * i + (pair + 1))
                    pe.wait_ge(sem["sb_stored"], 4 * i + (u + 3))
                    for t in range(TT):
                        mm = nc.tensor.matmul(ps[:, 4 * e + t, t * P:T], k_st_s[rows, pair, t * P:(t + 1) * P],
                                              q_st[rows, pair, t * P:T], start=True, stop=True)
                    mm.then_inc(sem["z_done"], 1)

                def rest(u):
                    pair, e = u // 2, u % 2
                    pe.wait_ge(sem["sp_ready"], 4 * i + (u + 1))
                    for t in range(TT):
                        b = 4 * e + t
                        nc.tensor.matmul(ps[:, b, t * P:T], con("neg_tri"), sp_b[:, e, CUT[t]:CUT[t + 1]],
                                         start=False, stop=False, skip_group_check=True)
                        for t2 in range(t + 1, TT):
                            nc.tensor.matmul(ps[:, b, t2 * P:T], con("neg_ones"), sp_b[:, e, CUT[t2]:CUT[t2 + 1]],
                                             start=False, stop=False, skip_group_check=True)
                        mm = nc.tensor.matmul(ps[:, b, t * P:(t + 1) * P], ident, con("sb_neg"),
                                              start=False, stop=True, skip_group_check=True)
                    mm.then_inc(sem["later_done"], 1)
                    pe.wait_ge(sem["w_done"], 4 * i + (u + 1))
                    for t in range(TT):
                        mm = nc.tensor.matmul(ps[64 * e:64 * e + 64, 4 * e, t * P:T], v_st[:, pair, t, 64 * e:64 * e + 64],
                                              wb[:, e, CUT[t]:CUT[t + 1]], start=(t == 0), stop=(t == TT - 1))
                    mm.then_inc(sem["pv_done"], 1)

                z_mm(0)
                for u in range(4):
                    if u < 3:
                        z_mm(u + 1)
                    rest(u)
            B()
            project_pe(pe, "sb_out", hn, ("res_added", 0))
            B()

            ffn_pe("ffn2", 0, 1)

            norm_pe(pe, hn)
            B()
            project_pe(pe, "kv_t", hn, ("proj_copied", 40))
            project_v_pe(pe, "kv_v", 16)
            B()
            pe.wait_ge(sem["xb_ready"], 1)
            for c in range(2):
                for m in range(16):
                    j = m // 4
                    pe.wait_ge(landed[j], 16 * (first["cmp_w1"] // RING + 1 + c))
                    for mt in range(2):
                        at = ((m % 4) * 2 + mt) * P
                        mm = nc.tensor.matmul(ps[:, 2 * c + mt, 0:124], ring[:, j, at:at + P], xb[:, c, m, :],
                                              start=(m == 0), stop=(m == 15), skip_group_check=True)
                    if m % 4 == 3:
                        mm.then_inc(sem["slots_used"], 1)
            pe.wait_ge(sem["cmp_silu"], 4)
            for mt in range(2):
                mm = nc.tensor.matmul(ps[0:64, 4, 0:124], con("w2_k")[:, mt * 64:(mt + 1) * 64], hid_c[:, 0, mt, :],
                                      start=(mt == 0), stop=(mt == 1))
            for g in range(KV_HEADS):
                for mt in range(2):
                    mm = nc.tensor.matmul(ps[0:N_CMP, 5, g * HD:(g + 1) * HD],
                                          hid_c[:, 1, mt, g * N_CMP:(g + 1) * N_CMP],
                                          con("w2_v")[:, mt * 64:(mt + 1) * 64], start=(mt == 0), stop=(mt == 1))
            mm.then_inc(sem["cmp_out"], 1)

            def head_pe(sq, xn, rows, cols, n):
                pe.wait_ge(sem["hr_squares"], n + 1)
                nc.tensor.matmul(ps[0:rows, 0, 0:cols], con("halves")[0:rows, 0:rows], sq[0:rows, 0:cols],
                                 start=True, stop=True).then_inc(sem["hr_sums"], 1)
                pe.wait_ge(sem["hr_normed"], n + 2)
                nc.tensor.matmul(ps[0:rows, 1, 0:cols], con("rot")[0:rows, 0:rows], xn[0:rows, 0:cols],
                                 start=True, stop=True).then_inc(sem["hr_rotated"], 1)

            head_pe(hr_sq, hr_xn, 64, 124, 0)
            for m in range(4):
                head_pe(hr_sq, hr_xn, P, T, 1 + m)
            B()

            ffn_pe("ffn1", 1, 2)

            norm_pe(pe, hn)
            B()
            project_pe(pe, "nsa_q", hn, ("proj_copied", 48))
            for t in range(TT):
                for k in range(DT):
                    mm = nc.tensor.matmul(ps[:, 6, t * 48:(t + 1) * 48], hn[:, k, t * P:(t + 1) * P],
                                          con("w_gates")[:, k * 48:(k + 1) * 48], start=(k == 0), stop=(k == DT - 1))
            mm.then_inc(sem["gates_mm"], 1)
            B()
            with pe.Fori(0, 8) as m:
                head_pe(hr2_sq, hr2_xn, P, T, m + 5)
            B()
            with pe.Fori(0, SB_PAIRS) as p:
                def z_mm(u):
                    e, br = u // 3, u % 3
                    bank = 4 * (u % 2)
                    if u % 3 == 0:
                        pe.wait_ge(sem["q_static"], 2 * p + (e + 1))
                    pe.wait_ge(sem["combined"], 6 * p + (u + 3))
                    for t in range(TT):
                        q = q_s2[0:64, e, t * P:(t + 1) * P]
                        if br < 2:
                            whole, own = ps[:, bank + t, 0:(t + 1) * P], ps[:, bank + t, t * P:(t + 1) * P]
                            mask, keys = con("causal_neg"), k_sw[0:64, p // 2 + 4 * br, 0:(t + 1) * P]
                        else:
                            whole = own = ps[:, bank, t * N_CMP:(t + 1) * N_CMP]
                            mask, keys = con("neg_c")[:, t * N_CMP:(t + 1) * N_CMP], k_c3[0:64, p // 2, :]
                        if t == 0:
                            nc.tensor.matmul(own, ident, mask, start=True, stop=False)
                            mm = nc.tensor.matmul(whole, q, keys, start=False, stop=True)
                        else:
                            nc.tensor.matmul(whole, q, keys, start=True, stop=False)
                            mm = nc.tensor.matmul(own, ident, mask, start=False, stop=True)
                    mm.then_inc(sem["z2_done"], 1)

                def rest(u):
                    e, br = u // 3, u % 3
                    b, bank = u % 2, 4 * (u % 2)
                    pe.wait_ge(sem["probs_ready"], 6 * p + (u + 1))
                    if br < 2:
                        for t2 in range(TT):
                            for t in range(t2, TT):
                                off = P * (t * (t + 1) // 2 + t2)
                                mm = nc.tensor.transpose(ps[:, bank + t2, t * P:(t + 1) * P], pr[:, b, off:off + P], ident)
                    else:
                        for t in range(TT):
                            mm = nc.tensor.transpose(ps[0:N_CMP, bank + 1, t * P:(t + 1) * P],
                                                     pr[:, b, t * N_CMP:(t + 1) * N_CMP], ident)
                    mm.then_inc(sem["turned"], 1)
                    wait_alone(pe, "turned_copied", 6 * p + (u + 1))
                    for t in range(TT):
                        o = ps[:, bank, t * HD:(t + 1) * HD]
                        if br < 2:
                            for t2 in range(t + 1):
                                at = CUT[t2] + (t - t2) * P
                                mm = nc.tensor.matmul(o, prt[:, b, at:at + P],
                                                      v_sw4[:, t2, p // 2 + 4 * br, :], start=(t2 == 0), stop=(t2 == t))
                        else:
                            mm = nc.tensor.matmul(o, prt[0:N_CMP, b, t * P:(t + 1) * P],
                                                  v_c3[0:N_CMP, p // 2, :], start=True, stop=True)
                    mm.then_inc(sem["attended"], 1)

                z_mm(0)
                for u in range(6):
                    if u < 5:
                        z_mm(u + 1)
                    rest(u)
            B()
            for k in range(DT):
                if k >= 4:
                    pe.wait_ge(sem["mix_copied"], k - 3)
                for t in range(TT):
                    mm = nc.tensor.transpose(ps[:, k % 4, t * P:(t + 1) * P], o_n[:, t, k * P:(k + 1) * P], ident)
                mm.then_inc(sem["mix_turned"], 1)
            B()
            project_pe(pe, "nsa_out", hn, ("res_added", 8))
            B()
            ffn_pe("ffn2", 1, 3)

        @block.scalar
        def _(act):
            B = lambda: barrier(act, "act")
            act.sem_inc(sem["even_copied"], RING)
            act.sem_inc(sem["gates_read"], 1)
            act.sem_inc(sem["even_out_copied"], 2)
            act.sem_inc(sem["proj_copied"], RING)
            act.wait_ge(sem["const_landed"], 16)
            act.wait_ge(sem["x_landed"], 16)
            nc.scalar.activation(lt[:, 0, :], con("lam"), ACT.Abs)
            act.drain()
            nc.scalar.activation(lt[:, 1, :], lt[:, 0, :], ACT.Exp, scale=-1.0)
            norm_act(act, res_flat, hn_flat)
            B()
            with act.Fori(0, RG_HEADS // 2) as i:
                for jj in range(2):
                    act.wait_ge(sem["even_channel_done"], 2 * i + (jj + 1))
                    dsts = [(xa_pad[:, jj, 2:2 + T], ACT.Copy), (xb_s[:, jj, :], ACT.Copy), (gc_s[:, jj, :], ACT.Copy),
                            (gb_s[:, jj, :], ACT.Copy), (szb[:, jj, :], ACT.Silu), (sza[:, jj, :], ACT.Silu)]
                    for n, (dst, func) in enumerate(dsts):
                        s = 6 * jj + n
                        act.wait_ge(sem["slots_used"], 12 * i + (s + 1 + RING))
                        nc.scalar.activation(dst, ps[:, s % RING, :], func).then_inc(sem["even_copied"], 1)
                    par = gw[:, jj, 4 * P:4 * P + 16]
                    act.wait_ge(sem["gates_done"], 2 * i + (jj + 1))
                    for d in range(2):
                        nc.scalar.activation(rg[:, d, :], ps[:, 4 + 2 * d, :], ACT.Sigmoid, bias=par[:, 2 * d:2 * d + 1])
                        a = nc.scalar.activation(ig[:, d, :], ps[:, 5 + 2 * d, :], ACT.Sigmoid,
                                                 bias=par[:, 2 * d + 1:2 * d + 2])
                    a.then_inc(sem["gates_read"], 1)
                    act.drain()
                    for d in range(2):
                        nc.scalar.activation(ag[:, d, :], rg[:, d, :], ACT.Exp, scale=nsp_c[:, jj, d:d + 1])
                    for d in range(2):
                        a = nc.scalar.activation(hg[:, d, :], rg[:, d, :], ACT.Tanh, scale=nsp_c[:, jj, d:d + 1])
                    a.then_inc(sem["decay_ready"], 1)
                    for d in range(2):
                        act.wait_ge(sem["factor_ready"], 4 * i + (2 * jj + d + 1))
                        nc.scalar.activation(rg[:, d, :], tg[:, d, :], ACT.Sqrt, scale=-1.0)\
                            .then_inc(sem["root_b_ready"], 1)
            B()
            copy_out_act(act, "even_out", ("even_out_copied", 0), ytmp, per_tile=2)
            B()
            norm_act(act, ytmp_flat, hn_flat)
            B()

            norm_act(act, res_flat, hn_flat)
            B()
            with act.Fori(0, 2) as i:
                for t in range(RING):
                    act.wait_ge(sem["slots_used"], used("odd_qkr", RING * i + (t + 1)))
                    nc.scalar.activation(qk_o[:, RING * i + t, :], ps[:, t, :], ACT.Copy).then_inc(sem["proj_copied"], 1)
            with act.Fori(0, 2) as i:
                for t in range(RING):
                    act.wait_ge(sem["slots_used"], used("odd_qkr", RING * i + (t + 9)))
                    nc.scalar.activation(r_o[:, RING * i + t, :], ps[:, t, :], ACT.Silu).then_inc(sem["proj_copied"], 1)
            act.wait_ge(sem["lr_done"], 1)
            nc.scalar.activation(lr_t[0:32, :], ps[0:32, 7, :], ACT.Copy).then_inc(sem["lr_copied"], 1)
            copy_v_act(act, "odd_v", v_o)
            B()
            with act.Fori(0, GLA_HEADS) as h:
                act.preload_act_table_set(LOG_SET)
                act.wait_ge(sem["gate_done"], h + 1)
                act.wait_ge(sem["gate_inputs"], h + 1)
                for d in range(2):
                    nc.scalar.activation(zb_o[:, d, :], ps[:, d, :], ACT.Identity, bias=bz[:, d:d + 1])
                act.drain()
                nc.scalar.activation(e_t[:, :, :], zb_o[:, :, :], ACT.Abs)
                act.drain()
                nc.scalar.activation(e_p[:, :, :], e_t[:, :, :], ACT.Exp, scale=-1.0)
                act.drain()
                nc.scalar.activation(e_n[:, :, :], e_p[:, :, :], ACT.Ln, bias=1.0).then_inc(sem["gate_log"], 1)
                act.wait_ge(sem["cum_ready"], h + 1)
                nc.scalar.activation(e_p[:, :, :], bc[:, :, :], ACT.Exp, scale=1.0 / 16)
                nc.scalar.activation(e_n[:, :, :], bc[:, :, :], ACT.Exp, scale=-1.0 / 16)
                nc.scalar.activation(e_t[:, :, :], k_st[:, :, :], ACT.Exp, scale=1.0 / 16).then_inc(sem["exps_ready"], 1)
                act.wait_ge(sem["scores_done"], h + 1)
                for d in range(2):
                    a = nc.scalar.activation(kstn[:, d, :], ps[:, 4 + d, :], ACT.Copy)
                a.then_inc(sem["kst_copied"], 1)
                act.wait_ge(sem["o_done"], h + 1)
                for t in range(TT):
                    nc.scalar.activation(kstn[:, t % 2, (t // 2) * 256:(t // 2) * 256 + 256], ps[:, t, 0:GLA_DV],
                                         ACT.Square, accum_out=ssum[:, t:t + 1])
                act.drain()
                nc.scalar.activation(sroot, ssum, ACT.Sqrt, bias=eps, scale=1.0 / GLA_DV).then_inc(sem["o_squared"], 1)
            B()
            copy_out_act(act, "odd_out", ("proj_copied", 0), ytmp_o)
            B()
            norm_act(act, ytmp_o_flat, hn_flat)
            B()

            def ffn_act(which, layer, nth):
                norm_act(act, res_flat, hn_flat)
                B()
                name = f"{which}_in_{layer}"
                with act.Fori(0, FT // 2) as i:
                    for j in range(2):
                        act.wait_ge(sem["hidden_ready"], 2 * i + (FT * nth + j + 1))
                        act.wait_ge(sem["slots_used"], used(name, 4 * i + (2 * j + 1)))
                        nc.scalar.activation(silu_a[:, j, :], ps[:, 2 * j, :], ACT.Silu).then_inc(sem["silu_done"], 1)
                B()
                B()

            ffn_act("ffn1", 0, 0)

            norm_act(act, res_flat, hn_flat)
            B()
            with act.Fori(0, 2) as i:
                for t in range(RING):
                    act.wait_ge(sem["slots_used"], used("sb_qk", RING * i + (t + 1)))
                    nc.scalar.activation(qk_s[:, RING * i + t, :], ps[:, t, :], ACT.Copy, scale=HD ** -0.5)\
                        .then_inc(sem["proj_copied"], 1)
            with act.Fori(0, 2) as i:
                for t in range(RING):
                    act.wait_ge(sem["slots_used"], used("sb_qk", RING * i + (t + 9)))
                    nc.scalar.activation(qk_s[:, RING * i + (t + 8), :], ps[:, t, :], ACT.Copy)\
                        .then_inc(sem["proj_copied"], 1)
            copy_v_act(act, "sb_v", v_s)
            B()
            act.preload_act_table_set(LOG_SET)
            with act.Fori(0, SB_PAIRS // 2) as i:
                def logs(u):
                    e = u % 2
                    act.wait_ge(sem["z_done"], 4 * i + (u + 1))
                    for t in range(TT):
                        nc.scalar.activation(lg[:, e, CUT[t]:CUT[t + 1]], ps[:, 4 * e + t, t * P:T], ACT.Abs)
                    act.drain()
                    nc.scalar.activation(lg[:, e, :], lg[:, e, :], ACT.Exp, scale=-1.0)
                    act.drain()
                    nc.scalar.activation(lg[:, e, :], lg[:, e, :], ACT.Ln, bias=1.0).then_inc(sem["log_done"], 1)

                def weigh(u):
                    e = u % 2
                    act.wait_ge(sem["later_done"], 4 * i + (u + 1))
                    for t in range(TT):
                        a = nc.scalar.activation(wb[:, e, CUT[t]:CUT[t + 1]], ps[:, 4 * e + t, t * P:T], ACT.Exp)
                    a.then_inc(sem["w_done"], 1)

                logs(0)
                for u in range(4):
                    if u < 3:
                        logs(u + 1)
                    weigh(u)
            B()
            B()

            ffn_act("ffn2", 0, 1)

            norm_act(act, res_flat, hn_flat)
            B()
            copy_out_act(act, "kv_t", ("proj_copied", 0), kt8)
            copy_v_act(act, "kv_v", v_sw)
            B()
            act.wait_ge(sem["slots_used"], used("cmp_w1", 8))
            for c in range(2):
                for mt in range(2):
                    nc.scalar.activation(hid_c[:, c, mt, :], ps[:, 2 * c + mt, 0:124], ACT.Silu)\
                        .then_inc(sem["cmp_silu"], 1)
            act.wait_ge(sem["cmp_out"], 1)
            nc.scalar.activation(kc_raw[0:64, :], ps[0:64, 4, 0:124], ACT.Copy)
            nc.scalar.activation(v_c[0:N_CMP, :], ps[0:N_CMP, 5, 0:256], ACT.Copy)
            act.drain().then_inc(sem["cmp_copied"], 1)

            def head_act(src, sq, rows, cols, n):
                nc.scalar.activation(sq[0:rows, 0:cols], src, ACT.Square).then_inc(sem["hr_squares"], 1)
                act.wait_ge(sem["hr_sums"], n + 1)
                act.wait_ge(sem["hr_normed"], n + 1)
                nc.scalar.activation(root[0:rows, 0:cols], ps[0:rows, 0, 0:cols], ACT.Sqrt, bias=eps[0:rows, :],
                                     scale=1.0 / HD).then_inc(sem["hr_root"], 1)

            head_act(kc_raw[0:64, :], hr_sq, 64, 124, 0)
            for m in range(4):
                head_act(kt8[:, 4 + m, :], hr_sq, P, T, 1 + m)
            B()

            ffn_act("ffn1", 1, 2)

            norm_act(act, res_flat, hn_flat)
            B()
            copy_out_act(act, "nsa_q", ("proj_copied", 0), q_t)
            act.wait_ge(sem["gates_mm"], 1)
            nc.scalar.activation(gts.rearrange("p t g -> p (t g)"), ps[:, 6, 0:192], ACT.Sigmoid)
            B()
            with act.Fori(0, 8) as m:
                head_act(q_t[:, m, :], hr2_sq, P, T, m + 5)
            B()
            with act.Fori(0, SB_PAIRS) as p:
                def probs(u):
                    br, b, bank = u % 3, u % 2, 4 * (u % 2)
                    act.wait_ge(sem["max_ready"], 6 * p + (u + 1))
                    for t in range(TT):
                        if br < 2:
                            off = P * (t * (t + 1) // 2)
                            dst, src = pr[:, b, off:off + (t + 1) * P], ps[:, bank + t, 0:(t + 1) * P]
                        else:
                            dst, src = pr[:, b, t * N_CMP:(t + 1) * N_CMP], ps[:, bank, t * N_CMP:(t + 1) * N_CMP]
                        nc.scalar.activation(dst, src, ACT.Exp, bias=zmax[:, b, t:t + 1], scale=HD ** -0.5,
                                             accum_out=psm[:, b, t:t + 1])
                    act.drain().then_inc(sem["probs_ready"], 1)

                def turn(u):
                    br, b, bank = u % 3, u % 2, 4 * (u % 2)
                    act.wait_ge(sem["turned"], 6 * p + (u + 1))
                    if br < 2:
                        for t in range(TT):
                            a = nc.scalar.activation(prt[:, b, CUT[t]:CUT[t + 1]], ps[:, bank + t, t * P:T], ACT.Copy)
                    else:
                        a = nc.scalar.activation(prt[0:N_CMP, b, 0:T], ps[0:N_CMP, bank + 1, :], ACT.Copy)
                    a.then_inc(sem["turned_copied"], 1)

                for u in range(6):
                    probs(u)
                    turn(u)
            B()
            for k in range(DT):
                act.wait_ge(sem["mix_turned"], k + 1)
                nc.scalar.activation(hn[:, k, :], ps[:, k % 4, :], ACT.Copy).then_inc(sem["mix_copied"], 1)
            B()
            B()
            ffn_act("ffn2", 1, 3)

        @block.vector
        def _(dve):
            B = lambda: barrier(dve, "dve")
            V = nc.vector
            dve.sem_inc(sem["even_channel_done"], 2)
            dve.sem_inc(sem["hidden_ready"], 2)
            dve.sem_inc(sem["down_done"], 2)
            dve.sem_inc(sem["res_added"], RING)
            dve.sem_inc(sem["o_stored"], 1)
            dve.sem_inc(sem["sb_stored"], 4)
            dve.sem_inc(sem["hr_normed"], 1)
            dve.sem_inc(sem["combined"], 4)
            dve.wait_ge(sem["const_landed"], 16)
            dve.wait_ge(sem["x_landed"], 16)
            for jj in range(2):
                V.memset(xa_pad[:, jj, 0:2], 0.0)
                V.memset(xa_pad[:, jj, 2 + T:3 + T], 0.0)
            V.memset(u_pad[:, 0:1], 0.0)
            V.memset(u_pad[:, 1 + T:2 + T], 0.0)
            dve.wait_ge(sem["squares_ready"], 1)
            V.tensor_scalar(lt[:, 2, :], lt[:, 1, :], 2.0, None, ALU.add)
            dve.drain()
            V.reciprocal(lt[:, 3, :], lt[:, 2, :])
            dve.drain()
            V.tensor_tensor(lt[:, 2, :], lt[:, 1, :], lt[:, 3, :], ALU.mult)
            dve.drain()
            V.tensor_tensor(lt[:, 3, :], lt[:, 2, :], lt[:, 2, :], ALU.mult)
            V.memset(lt[:, 4, :], 1.0 / 19)
            dve.drain()
            for odd in range(17, -1, -2):
                V.tensor_tensor(lt[:, 5, :], lt[:, 4, :], lt[:, 3, :], ALU.mult)
                dve.drain()
                V.tensor_scalar(lt[:, 4, :], lt[:, 5, :], 1.0 / odd, None, ALU.add)
                dve.drain()
            V.tensor_tensor(lt[:, 5, :], lt[:, 4, :], lt[:, 2, :], ALU.mult)
            V.tensor_scalar(lt[:, 3, :], con("lam"), -1.0, 0.0, ALU.mult, ALU.max)
            dve.drain()
            V.scalar_tensor_tensor(lt[:, 4, :], lt[:, 5, :], 2.0, lt[:, 3, :], ALU.mult, ALU.add)
            dve.drain()
            V.tensor_scalar(nsp, lt[:, 4, :], -8.0, None, ALU.mult)
            norm_dve(dve, res, "g_even_pre", hn)
            B()
            nsp2 = nsp.rearrange("p (c d) -> p c d", d=2)
            with dve.Fori(0, RG_HEADS // 2) as i:
                for jj in range(2):
                    par = gw[:, jj, 4 * P:4 * P + 16]
                    dve.wait_ge(gate_landed[jj], 16 * i + 16)
                    V.tensor_copy(nsp_c[:, jj, :], nsp2[:, 2 * i + jj, :])
                    dve.wait_ge(sem["even_copied"], 12 * i + (6 * jj + 1 + RING))
                    V.tensor_scalar(ua[:, jj, :], xa_pad[:, jj, 0:T], par[:, 4:5], par[:, 8:9], ALU.mult, ALU.add)
                    for k in range(1, 4):
                        dve.drain()
                        op = V.scalar_tensor_tensor(ua[:, jj, :], xa_pad[:, jj, k:k + T], par[:, 4 + k:5 + k],
                                                    ua[:, jj, :], ALU.mult, ALU.add)
                    op.then_inc(sem["ua_ready"], 1)
                    dve.wait_ge(sem["even_copied"], 12 * i + (6 * jj + 3 + RING))
                    V.tensor_tensor(u_pad[:, 1:1 + T], gc_s[:, jj, :], xb_s[:, jj, :], ALU.mult)
                    dve.drain()
                    V.tensor_scalar(cv, u_pad[:, 0:T], par[:, 9:10], None, ALU.mult)
                    for k in range(1, 3):
                        dve.drain()
                        V.scalar_tensor_tensor(cv, u_pad[:, k:k + T], par[:, 9 + k:10 + k], cv, ALU.mult, ALU.add)
                    dve.drain()
                    dve.wait_ge(sem["even_copied"], 12 * i + (6 * jj + 6 + RING))
                    V.tensor_tensor(cv, cv, gb_s[:, jj, :], ALU.mult)
                    dve.drain()
                    V.tensor_tensor(y_even[:, 2 * i + (jj + 8), :], cv, szb[:, jj, :], ALU.mult)
                    dve.wait_ge(sem["decay_ready"], 2 * i + (jj + 1))
                    for d in range(2):
                        V.tensor_tensor(tg[:, d, :], ag[:, d, :], ag[:, d, :], ALU.mult)
                        dve.drain()
                        V.scalar_tensor_tensor(tg[:, d, :], tg[:, d, :], 1.0, hg[:, d, :], ALU.add, ALU.mult)\
                            .then_inc(sem["factor_ready"], 1)
                        V.tensor_tensor(ig[:, d, :], ig[:, d, :], ua[:, jj, :], ALU.mult)
                    for d in range(2):
                        dve.drain()
                        dve.wait_ge(sem["root_b_ready"], 4 * i + (2 * jj + d + 1))
                        V.tensor_tensor(tg[:, d, :], ig[:, d, :], rg[:, d, :], ALU.mult)
                        dve.drain()
                        way = slice(None, None, 1 if d == 0 else -1)
                        V.tensor_tensor_scan(hg[:, d, way], ag[:, d, way], tg[:, d, way], 0.0, ALU.mult, ALU.add)
                    dve.drain()
                    V.tensor_tensor(tg[:, 0, :], hg[:, 0, :], hg[:, 1, :], ALU.add)
                    dve.drain()
                    V.tensor_tensor(y_even[:, 2 * i + jj, :], tg[:, 0, :], sza[:, jj, :], ALU.mult)\
                        .then_inc(sem["even_channel_done"], 1)
            B()
            B()

            def post_norm(y, y_flat, gain):
                norm_dve(dve, y, gain, y)
                dve.drain()
                V.tensor_tensor(res_flat, res_flat, y_flat, ALU.add)

            post_norm(ytmp, ytmp_flat, "g_even_post")
            B()

            norm_dve(dve, res, "g_odd_pre", hn)
            B()
            V.memset(st[:, :, :], 0.0)
            B()
            gla_keep = con("gla_keep").rearrange("p (d t) -> p d t", d=2).bitcast(U32)
            chunk_keep = con("chunk_keep").rearrange("p (d t) -> p d t", d=2)
            with dve.Fori(0, GLA_HEADS) as h:
                dve.wait_ge(sem["gate_log"], h + 1)
                V.scalar_tensor_tensor(la_o[:, :, :], zb_o[:, :, :], 0.0, e_n[:, :, :], ALU.min, ALU.subtract)
                dve.drain()
                for d in range(2):
                    way = slice(None, None, 1 if d == 0 else -1)
                    V.tensor_tensor_scan(bc[:, d, way], chunk_keep[:, d, way], la_o[:, d, way], 0.0, ALU.mult, ALU.add)
                dve.drain()
                for d in range(2):
                    b3 = bc[:, d, :].rearrange("p (n t) -> p n t", t=GLA_CHUNK)
                    end = GLA_CHUNK - 1 if d == 0 else 0
                    op = V.tensor_tensor(k_st[:, d, :].rearrange("p (n t) -> p n t", t=GLA_CHUNK),
                                         b3[:, :, end:end + 1].to_broadcast([P, GLA_NCH, GLA_CHUNK]), b3, ALU.subtract)
                op.then_inc(sem["cum_ready"], 1)
                dve.wait_ge(sem["exps_ready"], h + 1)
                for d in range(2):
                    V.scalar_tensor_tensor(q_in[:, d, :], qk_o[:, h, :], float(GLA_DK) ** -0.5, e_p[:, d, :],
                                           ALU.mult, ALU.mult)
                    V.tensor_tensor(k_in[:, d, :], qk_o[:, h + 4, :], e_n[:, d, :], ALU.mult)
                    op = V.tensor_tensor(k_st[:, d, :], qk_o[:, h + 4, :], e_t[:, d, :], ALU.mult)
                op.then_inc(sem["qk_scaled"], 1)
                wait_alone(dve, "scores_done", h + 1)
                for d in range(2):
                    op = V.copy_predicated(st[:, d, :], gla_keep[:, d, :], ps[:, 2 + d, :])
                op.then_inc(sem["scores_masked"], 1)
                dve.wait_ge(sem["updates_done"], h + 1)
                for step in range(GLA_NCH - 1):
                    if step > 0:
                        dve.drain()
                    for d in range(2):
                        n = step if d == 0 else GLA_NCH - 1 - step
                        nxt = n + (1 if d == 0 else -1)
                        upd = update_of(d, n)
                        edge = n * GLA_CHUNK + (GLA_CHUNK - 1 if d == 0 else 0)
                        if step == 0:
                            op = V.tensor_copy(states[:, d, nxt, :], upd)
                        else:
                            op = V.scalar_tensor_tensor(states[:, d, nxt, :], states[:, d, n, :],
                                                        e_p[:, d, edge:edge + 1], upd, ALU.mult, ALU.add)
                op.then_inc(sem["states_ready"], 1)
                dve.wait_ge(sem["o_squared"], h + 1)
                V.reciprocal(sinv, sroot)
                dve.drain()
                for t in range(TT):
                    op = V.tensor_scalar(on_o[:, t, :], ps[:, t, 0:GLA_DV], sinv[:, t:t + 1], None, ALU.mult)
                op.then_inc(sem["o_scaled"], 1)
                dve.wait_ge(sem["o_turned"], h + 1)
                for e in range(2):
                    op = V.scalar_tensor_tensor(hn[:, 2 * h + e, :], ps[:, 4 + e, :], con("gla_g")[:, e:e + 1],
                                                r_o[:, 2 * h + e, :], ALU.mult, ALU.mult)
                op.then_inc(sem["o_stored"], 1)
            B()
            B()
            post_norm(ytmp_o, ytmp_o_flat, "g_odd_post")
            B()

            def ffn_dve(which, layer, nth):
                norm_dve(dve, res, f"g_{which}_{layer}", hn)
                B()
                name = f"{which}_in_{layer}"
                with dve.Fori(0, FT // 2) as i:
                    for j in range(2):
                        dve.wait_ge(sem["silu_done"], 2 * i + (FT * nth + j + 1))
                        dve.wait_ge(sem["slots_used"], used(name, 4 * i + (2 * j + 2)))
                        V.tensor_tensor(hid[:, 2 * i + j, :], silu_a[:, j, :], ps[:, 2 * j + 1, :], ALU.mult)\
                            .then_inc(sem["hidden_ready"], 1)
                B()
                name = f"{which}_out_{layer}"
                with dve.Fori(0, 4) as i:
                    for t in range(2):
                        dve.wait_ge(sem["slots_used"], used(name, 4 * i + (2 * t + 2)))
                        V.scalar_tensor_tensor(res[:, 2 * i + t, :], ps[:, t, :], 0.5, res[:, 2 * i + t, :],
                                               ALU.mult, ALU.add).then_inc(sem["down_done"], 1)
                B()

            ffn_dve("ffn1", 0, 0)

            norm_dve(dve, res, "g_mix_0", hn)
            B()
            B()
            with dve.Fori(0, SB_PAIRS // 2) as i:
                def softplus(u):
                    e = u % 2
                    dve.wait_ge(sem["log_done"], 4 * i + (u + 1))
                    for t in range(TT):
                        V.scalar_tensor_tensor(sp_b[:, e, CUT[t]:CUT[t + 1]], ps[:, 4 * e + t, t * P:T], 0.0,
                                               lg[:, e, CUT[t]:CUT[t + 1]], ALU.max, ALU.add)
                    dve.drain()
                    for t in range(TT):
                        d = sp_b[:, e, CUT[t]:CUT[t] + P]
                        op = V.tensor_tensor(d, d, con("sb_keep"), ALU.mult)
                    op.then_inc(sem["sp_ready"], 1)

                def store(u):
                    pair, e = u // 2, u % 2
                    dve.wait_ge(sem["pv_done"], 4 * i + (u + 1))
                    V.tensor_copy(hn[64 * e:64 * e + 64, 2 * i + pair, :], ps[64 * e:64 * e + 64, 4 * e, :])\
                        .then_inc(sem["sb_stored"], 1)

                softplus(0)
                for u in range(4):
                    if u < 3:
                        softplus(u + 1)
                    store(u)
            B()

            with dve.Fori(0, 2) as i:
                for t in range(RING):
                    dve.wait_ge(sem["slots_used"], used("sb_out", RING * i + (t + 1)))
                    V.tensor_tensor(res[:, RING * i + t, :], ps[:, t, :], res[:, RING * i + t, :], ALU.add)\
                        .then_inc(sem["res_added"], 1)
            B()

            ffn_dve("ffn2", 0, 1)

            norm_dve(dve, res, "g_kv", hn)
            B()
            B()
            for c in range(2):
                for g in range(KV_HEADS):
                    src = kt8[64 * (g % 2):64 * (g % 2) + 64, 2 * c + g // 2, :]
                    V.tensor_copy(x2[0:64, c, g, :], src)
                    V.tensor_copy(x2[64:128, c, g, 0:T - 1], src[:, 1:T])
            dve.drain()
            for c in range(2):
                pos = con("pos_k" if c == 0 else "pos_v")
                for m in range(16):
                    op = V.tensor_scalar(xb[:, c, m, :].rearrange("p (g n) -> p g n", g=KV_HEADS),
                                         x2[:, c, :, 2 * m:2 * m + 16 * (N_CMP - 1) + 1:16],
                                         pos[:, m:m + 1], None, ALU.add)
            op.then_inc(sem["xb_ready"], 1)

            def head_dve(src, xn, t1, t2, gain, rows, cols, cos, sin, dsts, n):
                dve.wait_ge(sem["hr_root"], n + 1)
                V.reciprocal(rinv[0:rows, 0:cols], root[0:rows, 0:cols])
                dve.drain()
                V.scalar_tensor_tensor(xn[0:rows, 0:cols], src, gain, rinv[0:rows, 0:cols], ALU.mult, ALU.mult)\
                    .then_inc(sem["hr_normed"], 1)
                dve.drain()
                V.tensor_tensor(t1[0:rows, 0:cols], xn[0:rows, 0:cols], cos, ALU.mult)
                dve.wait_ge(sem["hr_rotated"], n + 1)
                V.tensor_tensor(t2[0:rows, 0:cols], ps[0:rows, 1, 0:cols], sin, ALU.mult)
                dve.drain()
                for half, dst in enumerate(dsts):
                    V.tensor_tensor(dst, t1[64 * half:64 * half + 64, 0:cols], t2[64 * half:64 * half + 64, 0:cols],
                                    ALU.add)
                dve.drain()

            dve.wait_ge(sem["cmp_copied"], 1)
            head_dve(kc_raw[0:64, :], hr_xn, hr_t1, hr_t2, con("k_norm")[0:64, 0:1], 64, 124,
                     con("cos_c")[0:64, :], con("sin_c")[0:64, :], [k_c[0:64, :]], 0)
            for m in range(4):
                br, pair = m // 2, m % 2
                head_dve(kt8[:, 4 + m, :], hr_xn, hr_t1, hr_t2, con("k_norm")[:, 1 + br:2 + br], P, T,
                         con("cos"), con("sin"),
                         [k_sw[0:64, 4 * br + 2 * pair + half, :] for half in range(2)], 1 + m)
            B()

            ffn_dve("ffn1", 1, 2)

            norm_dve(dve, res, "g_mix_1", hn)
            B()
            B()
            for t in range(TT):
                V.tensor_scalar(gts[:, t, 0:16], gts[:, t, 0:16], con("valid")[:, t:t + 1], None, ALU.mult)
            with dve.Fori(0, 8) as m:
                head_dve(q_t[:, m, :], hr2_xn, hr2_t1, hr2_t2, con("q_norm"), P, T, con("cos"), con("sin"),
                         [q_h[0:64, 2 * m + half, :] for half in range(2)], m + 5)
            B()
            with dve.Fori(0, SB_PAIRS) as p:
                def maxima(u):
                    br, b, bank = u % 3, u % 2, 4 * (u % 2)
                    dve.wait_ge(sem["z2_done"], 6 * p + (u + 1))
                    if br < 2:
                        for t in range(TT):
                            V.tensor_reduce(coef[:, b, t:t + 1], ps[:, bank + t, 0:(t + 1) * P], AX, ALU.max)
                    else:
                        V.tensor_reduce(coef[:, b, :], ps[:, bank, 0:4 * N_CMP].rearrange("p (t n) -> p t n", t=TT),
                                        AX, ALU.max)
                    dve.drain()
                    V.tensor_scalar(zmax[:, b, :], coef[:, b, :], -(HD ** -0.5), None, ALU.mult)\
                        .then_inc(sem["max_ready"], 1)

                def combine(u):
                    e, br, b, bank = u // 3, u % 3, u % 2, 4 * (u % 2)
                    col = (16, 32, 0)[br]
                    dve.wait_ge(sem["attended"], 6 * p + (u + 1))
                    V.reciprocal(psm[:, b, :], psm[:, b, :])
                    dve.drain()
                    V.tensor_tensor(coef[:, b, :], psm[:, b, :], gts_g[:, 2 * p + (col + e), :], ALU.mult)
                    dve.drain()
                    for t in range(TT):
                        o = o_n4[:, t, 2 * p + e, :]
                        src = ps[:, bank, t * HD:(t + 1) * HD]
                        if br == 0:
                            op = V.tensor_scalar(o, src, coef[:, b, t:t + 1], None, ALU.mult)
                        else:
                            op = V.scalar_tensor_tensor(o, src, coef[:, b, t:t + 1], o, ALU.mult, ALU.add)
                    op.then_inc(sem["combined"], 1)
                    dve.drain()

                maxima(0)
                for u in range(6):
                    if u < 5:
                        maxima(u + 1)
                    combine(u)
            B()
            B()
            with dve.Fori(0, 2) as i:
                for t in range(RING):
                    dve.wait_ge(sem["slots_used"], used("nsa_out", RING * i + (t + 1)))
                    V.tensor_tensor(res[:, RING * i + t, :], ps[:, t, :], res[:, RING * i + t, :], ALU.add)\
                        .then_inc(sem["res_added"], 1)
            B()
            ffn_dve("ffn2", 1, 3)

        @block.gpsimd
        def _(pool):
            G = nc.gpsimd
            B = lambda: barrier(pool, "pool")
            pool.wait_ge(sem["const_landed"], 16)
            for _ in range(6):
                B()
            w_gate = con("w_gate_lr").rearrange("p (h d c) -> p h d c", h=GLA_HEADS, d=2)
            bias = con("gla_bias").rearrange("p (h d) -> p h d", d=2)
            v4 = v_o.rearrange("p t (h e) -> p t h e", h=GLA_HEADS)
            with pool.Fori(0, GLA_HEADS) as h:
                pool.wait_ge(sem["o_stored"], h + 1)
                G.tensor_copy(wz[0:32, :, :], w_gate[0:32, h, :, :])
                G.tensor_copy(bz, bias[:, h, :])
                G.tensor_copy(vh[:, :, :], v4[:, :, h, :])
                pool.drain().then_inc(sem["gate_inputs"], 1)
            for _ in range(8):
                B()
            qk4 = qk_s
            v3 = v_s.rearrange("p t (g d) -> p t g d", d=P)
            with pool.Fori(0, SB_PAIRS // 2) as i:
                for pair in range(2):
                    pool.wait_ge(sem["sb_stored"], 4 * i + (2 * pair + 2))
                    G.tensor_copy(q_st[:, pair, :], qk4[:, 2 * i + pair, :])
                    G.tensor_copy(k_st_s[:, pair, :], qk4[:, 2 * i + (pair + 8), :])
                    G.tensor_copy(v_st[:, pair, :, :], v3[:, :, 2 * i + pair, :])
                    pool.drain().then_inc(sem["sb_copies"], 1)
            for _ in range(14):
                B()
            with pool.Fori(0, SB_PAIRS) as p:
                for e in range(2):
                    pool.wait_ge(sem["combined"], 6 * p + (3 * e + 1))
                    G.tensor_copy(q_s2[0:64, e, :], q_h[0:64, 2 * p + e, :])
                    pool.drain().then_inc(sem["q_static"], 1)
            for _ in range(6):
                B()


def by_tiles(w):
    k, m = w.shape
    return w.reshape(k // P, P, m // P, P).transpose(2, 1, 0, 3).reshape(m // P, P, k)


def in_parts(w, parts):
    k, m = w.shape
    return w.reshape(parts, k // P // parts, P, m // P, P).transpose(3, 0, 2, 1, 4).reshape(m // P * parts, P, k // parts)


def by_columns(w):
    k, m = w.shape
    return w.reshape(4, 2, P, m // 512, 512).transpose(3, 0, 2, 1, 4).reshape(m // 128, P, 1024)


def col(v):
    return v.reshape(-1, P).T


def tables():
    f = np.float32
    t = {}
    a, b = np.arange(P)[:, None], np.arange(P)[None, :]
    t["ident"] = (a == b).astype(f)
    t["ones"] = np.ones((P, P), f)
    t["halves"] = (a // 64 == b // 64).astype(f)
    rot = np.zeros((P, P), f)
    for base in (0, 64):
        for d in range(8):
            rot[base + d + 8, base + d] = -1.0
            rot[base + d, base + d + 8] = 1.0
    t["rot"] = rot
    t["neg_tri"] = -(a >= b).astype(f)
    t["neg_ones"] = -np.ones((P, P), f)
    t["sb_neg"] = np.where(a >= b, NEG, 0.0).astype(f)
    t["sb_keep"] = (a < b).astype(f)
    t["causal_neg"] = np.where(b > a, NEG, 0.0).astype(f)
    same = a // GLA_CHUNK == b // GLA_CHUNK
    t["gla_keep"] = np.concatenate([np.tile((same & (a <= b)).astype(f), (1, TT)),
                                    np.tile((same & (a >= b)).astype(f), (1, TT))], 1)
    tok = np.arange(T)
    keep = np.stack([tok % GLA_CHUNK != 0, tok % GLA_CHUNK != GLA_CHUNK - 1]).astype(f)
    t["chunk_keep"] = np.broadcast_to(keep.reshape(1, 2 * T), (P, 2 * T))
    inv_freq = np.power(f(500000.0), -np.arange(0, 16, 2, dtype=f) / f(16)).astype(f)

    def rope(positions):
        ang = positions.astype(f)[None, :] * inv_freq[:, None]
        n = len(positions)
        c, s = np.ones((64, n), f), np.zeros((64, n), f)
        c[0:8] = c[8:16] = np.cos(ang)
        s[0:8] = s[8:16] = np.sin(ang)
        return np.concatenate([c, c]), np.concatenate([s, s])

    t["cos"], t["sin"] = rope(tok)
    ends = np.arange(N_CMP) * 16 + 31
    c, s = rope(ends)
    t["cos_c"], t["sin_c"] = np.tile(c, (1, KV_HEADS)), np.tile(s, (1, KV_HEADS))
    query = np.arange(TT)[None, :, None] * P + np.arange(P)[:, None, None]
    t["neg_c"] = np.where(ends[None, None, :] <= query, 0.0, NEG).astype(f).reshape(P, TT * N_CMP)
    t["valid"] = (query[:, :, 0] >= 31).astype(f)
    t["eps"] = np.full((P, 1), EPS, f)
    return t


def kernel(**inputs):
    import concourse.bacc as bacc
    from concourse.bass_utils import run_bass_kernel_spmd

    a = {k: np.asarray(v) for k, v in inputs.items()}
    c = tables()
    for name, v in (("even_pre", a["even_norm_pre"][0]), ("even_post", a["even_norm_post"][0]),
                    ("odd_pre", a["odd_norm_pre"][0]), ("odd_post", a["odd_norm_post"][0]),
                    ("ffn1_0", a["ffn1_norm_2"][0]), ("ffn1_1", a["ffn1_norm_2"][1]),
                    ("mix_0", a["mix_norm_2"][0]), ("mix_1", a["mix_norm_2"][1]),
                    ("ffn2_0", a["ffn2_norm_2"][0]), ("ffn2_1", a["ffn2_norm_2"][1]), ("kv", a["kv_norm_2"])):
        c["g_" + name] = col(v)
    c["lam"] = a["rg_lambda"][0].reshape(2, RG_HEADS, P).transpose(2, 1, 0).reshape(P, 16)
    c["gla_bias"] = a["gla_b_gate"][0].reshape(2, GLA_HEADS, P).transpose(2, 1, 0).reshape(P, 8)
    c["gla_g"] = col(a["gla_norm_g"][0])
    c["q_norm"] = np.tile(a["nsa_q_norm_2"][0], 2).reshape(P, 1)
    c["k_norm"] = np.tile(a["nsa_k_norm_2"].T, (2, 1))
    c["pos_k"] = a["cmp_pos_k_2"].reshape(16, P).T
    c["pos_v"] = a["cmp_pos_v_2"].reshape(16, P).T
    w_odd = a["odd_w_in"][0]
    c["w_lr"] = w_odd[:, 3072:3104].reshape(DT, P, 32).transpose(1, 0, 2).reshape(P, 256)
    gate_lr = np.zeros((P, GLA_HEADS, 2, P), np.float32)
    for d in range(2):
        gate_lr[d * GLA_RANK:(d + 1) * GLA_RANK, :, d, :] = a["gla_w_gate_lr"][0, d].reshape(GLA_RANK, GLA_HEADS, P)
    c["w_gate_lr"] = gate_lr.reshape(P, -1)
    c["w2_k"] = a["cmp_k_w2_2"].reshape(2, P, HD).transpose(1, 0, 2).reshape(P, 128)
    c["w2_v"] = a["cmp_v_w2_2"].reshape(2, P, HD).transpose(1, 0, 2).reshape(P, 128)
    w_nsa = a["nsa_w_in_2"][0]
    c["w_gates"] = w_nsa[:, D:].reshape(DT, P, 48).transpose(1, 0, 2).reshape(P, 384)
    consts = np.concatenate([np.asarray(c[name], np.float32).reshape(P, n) for name, n in CONSTS], 1)

    gates = np.zeros((RG_HEADS, P, GATE_COLS), np.float32)
    gates[:, :, 0:4 * P] = a["rg_gate_w"][0].reshape(4, RG_HEADS, P, P).transpose(1, 2, 0, 3).reshape(RG_HEADS, P, 4 * P)
    gates[:, :, 4 * P:4 * P + 4] = a["rg_gate_b"][0].reshape(4, RG_HEADS, P).transpose(1, 2, 0)
    gates[:, :, 4 * P + 4:4 * P + 8] = a["rg_conv_w"][0].reshape(4, RG_HEADS, P).transpose(1, 2, 0)
    gates[:, :, 4 * P + 8] = a["rg_conv_b"][0].reshape(RG_HEADS, P)
    gates[:, :, 4 * P + 9:4 * P + 12] = a["sc_conv_w"][0].reshape(3, RG_HEADS, P).transpose(1, 2, 0)

    w = {}
    ev = by_tiles(a["even_w_in"][0]).reshape(6, DT, P, D)
    w["even_in"] = ev[[0, 2, 4, 3, 5, 1]].transpose(1, 0, 2, 3).reshape(48, P, D)
    w["even_out"] = in_parts(a["even_w_out"][0], 2)
    w["odd_qkr"] = by_tiles(np.concatenate([w_odd[:, 0:1024], w_odd[:, 2048:3072]], 1))
    w["odd_v"] = by_columns(w_odd[:, 1024:2048])
    w["odd_out"] = by_tiles(a["odd_w_out"][0])
    for which in ("ffn1", "ffn2"):
        for layer in range(2):
            both = by_tiles(a[f"{which}_w_in_2"][layer]).reshape(2, FT, P, D)
            w[f"{which}_in_{layer}"] = both.transpose(1, 0, 2, 3).reshape(2 * FT, P, D)
            w[f"{which}_out_{layer}"] = in_parts(a[f"{which}_w_out_2"][layer], 2)
    qkv = a["sb_w_qkv_2"][0]
    w["sb_qk"], w["sb_v"] = by_tiles(qkv[:, 0:2048]), by_columns(qkv[:, 2048:3072])
    w["sb_out"] = by_tiles(a["sb_w_out_2"][0])
    kv = a["nsa_w_kv_2"]
    part = [kv[:, 256 * i:256 * (i + 1)] for i in range(6)]
    w["kv_t"] = by_tiles(np.concatenate([part[0], part[1], part[2], part[4]], 1))
    w["kv_v"] = by_columns(np.concatenate([part[3], part[5]], 1))
    w["cmp_w1"] = np.concatenate([a[n].reshape(4, 4, P, 2, P).transpose(0, 2, 1, 3, 4).reshape(4, P, 1024)
                                  for n in ("cmp_k_w1_2", "cmp_v_w1_2")], 0)
    w["nsa_q"] = by_tiles(w_nsa[:, 0:D])
    w["nsa_out"] = by_tiles(a["nsa_w_out_2"][0])

    arrays = {"x": a["x"][0].T.reshape(DT, P, T).transpose(1, 0, 2), "consts": consts, "gates": gates}
    arrays.update(w)
    arrays = {k: np.ascontiguousarray(v) for k, v in arrays.items()}
    nc = bacc.Bacc("TRN2", target_bir_lowering=False, num_devices=1)
    aps = {k: nc.dram_tensor(f"in_{k}", v.shape, F32, kind="ExternalInput").ap() for k, v in arrays.items()}
    out = nc.dram_tensor("out_y", (P, DT, T), F32, kind="ExternalOutput").ap()
    build(nc, aps["x"], aps["consts"], aps["gates"], {name: aps[name] for name, _, _ in STREAM}, out)
    got = run_bass_kernel_spmd(nc, [{f"in_{k}": v for k, v in arrays.items()}], core_ids=[0])
    y = got.results[0]["out_y"]
    return np.ascontiguousarray(y.transpose(2, 1, 0).reshape(1, T, D))
```

```python
from contextlib import ExitStack

import numpy as np
import concourse.bass as bass
from concourse import mybir

F32 = mybir.dt.float32
BF16 = mybir.dt.bfloat16
F32R = mybir.dt.float32r
U32 = mybir.dt.uint32
ACT = mybir.ActivationFunctionType
ALU = mybir.AluOpType
AX = mybir.AxisListType.X

P = 128
D = 1024
T = 512
DT = D // P
TT = T // P
EPS = 1e-6
RG_HEADS = 8
GLA_HEADS, GLA_DK, GLA_DV, GLA_RANK, GLA_CHUNK = 4, 128, 256, 16, 64
GLA_NCH = T // GLA_CHUNK
D_FF = 2816
FT = D_FF // P
HD = 64
SB_PAIRS = D // (2 * HD)
KV_HEADS = 4
N_CMP = (T - 32) // 16 + 1
NEG = -2.0 ** 100
RING = 4
HALVES = (12, 10)
SLOT = HALVES[0] * P
LOG_SET = "natural_log_exp_and_others"


def ffn_stream(which, layer):
    return [(f"{which}_{way}_{layer}_{half}", 2 * n if way == "in" else DT, (DT if way == "in" else n) * P)
            for half, n in enumerate(HALVES) for way in ("in", "out")]


STREAM = [
    ("even_in", 48, 8 * P), ("even_out", 16, 8 * P),
    ("odd_qk", 8, 8 * P), ("odd_r", 8, 8 * P), ("odd_v", 8, 8 * P), ("odd_out", 8, 8 * P),
    *ffn_stream("ffn1", 0),
    ("sb_q", 8, 8 * P), ("sb_k", 8, 8 * P), ("sb_v", 8, 8 * P), ("sb_out", 8, 8 * P),
    *ffn_stream("ffn2", 0),
    ("kv_t", 8, 8 * P), ("kv_v", 4, 8 * P), ("cmp_w1", 8, 8 * P),
    *ffn_stream("ffn1", 1),
    ("nsa_q", 8, 8 * P), ("nsa_out", 8, 8 * P),
    *ffn_stream("ffn2", 1),
]
SPLIT = [name for name, _, _ in STREAM if name != "cmp_w1"]

CONSTS = [
    ("g_even_pre", 8), ("g_even_post", 8), ("g_odd_pre", 8), ("g_odd_post", 8),
    ("g_ffn1_0", 8), ("g_ffn1_1", 8), ("g_mix_0", 8), ("g_mix_1", 8), ("g_ffn2_0", 8), ("g_ffn2_1", 8),
    ("g_kv", 8), ("lam", 16), ("gla_bias", 8), ("gla_g", 2), ("q_norm", 1), ("k_norm", 3),
    ("pos_k", 16), ("pos_v", 16), ("eps", 1), ("valid", 4),
    ("w_lr", 256), ("w_gate_lr", 1024), ("w2_k", 128), ("w2_v", 128), ("w_gates", 384),
    ("ident", 128), ("ones", 128), ("halves", 128), ("rot", 128), ("neg_tri", 128), ("neg_ones", 128),
    ("sb_neg", 128), ("sb_keep", 128), ("causal_neg", 128), ("gla_keep", 1024), ("chunk_keep", 1024),
    ("cos", 512), ("sin", 512), ("cos_c", 124), ("sin_c", 124), ("neg_c", 124),
]
CONST_AT = {}
_at = 0
for _name, _n in CONSTS:
    CONST_AT[_name] = (_at, _n)
    _at += _n
N_CONSTS = _at
GATE_COLS = 4 * P + 16

SIGNALS = """
x_landed const_landed out_stored phase_end slots_used high_ready low_ready hn_scaled hn_high hn_ready
squares_ready sumsq_ready root_ready
even_moved ua_ready gates_done gates_read decay_ready factor_ready root_b_ready even_channel_done
even_out_copied proj_copied v_copied lr_done lr_copied res_added
gate_inputs gate_done gate_read gate_log v_ready cum_ready exps_ready qk_scaled scores_done scores_masked kst_copied
updates_done states_ready o_done o_squared o_scaled o_turned o_stored
silu_done hidden_ready down_done
sb_copies sb_values z_done log_done sp_ready sums_ready later_done w_done pv_done sb_stored
hr_squares hr_sums hr_root hr_normed hr_rotated
xb_ready cmp_silu cmp_out cmp_copied gates_mm
q_static z2_done max_ready probs_ready turned first_turned rest_turned attended combined mix_turned mix_copied
""".split()


def build(nc, x_in, consts_in, gates_in, weights, out):
    ctx = ExitStack()
    with ctx:
        sem = {}
        for name in SIGNALS:
            sem[name] = ctx.enter_context(nc.semaphore(name))
        landed = [ctx.enter_context(nc.semaphore(f"slot_landed_{j}")) for j in range(RING)]
        gate_landed = [ctx.enter_context(nc.semaphore(f"gate_landed_{j}")) for j in range(2)]

        base = (nc.sbuf_base + 31) // 32 * 32
        place = {}
        end = [0]

        def put(name, cols):
            place[name] = end[0]
            end[0] += cols

        def at(name, cols, start, dt=F32):
            return nc.alloc_sbuf_tensor_at(name, [P, cols], dt, offset=base + 4 * start)

        def tiled(name, n, cols, start, dt=F32):
            return at(name, n * cols, start, dt)[:, :].rearrange("p (k t) -> p k t", t=cols)

        ARENA = 30632
        for name, cols in (("res", DT * T), ("hn", DT * T), ("ring", RING * SLOT), ("consts", (N_CONSTS + 7) // 8 * 8),
                           ("root", T), ("rinv", T), ("masks", 2 * P), ("arena", ARENA)):
            put(name, cols)
        res = tiled("res", DT, T, place["res"])
        hn = tiled("hn", DT, T, place["hn"])
        hn_flat = hn.rearrange("p k t -> p (k t)")
        res_flat = res.rearrange("p k t -> p (k t)")
        ring = tiled("ring", RING, SLOT, place["ring"])
        consts = at("consts", N_CONSTS, place["consts"])
        root, rinv = at("root", T, place["root"]), at("rinv", T, place["rinv"])
        arena = at("arena", ARENA, place["arena"])
        masks = at("masks", 4 * P, place["masks"], BF16)
        ident_1, causal_1, sb_neg_1 = (masks[:, n * P:(n + 1) * P] for n in range(3))
        neg_c_1 = masks[:, 3 * P:3 * P + TT * N_CMP]
        ps = ctx.enter_context(nc.psum_tensor("ps", [P, 8, 512], F32))

        def con(name):
            at, n = CONST_AT[name]
            return consts[:, at:at + n]

        ident, ones = con("ident"), con("ones")
        eps = con("eps")

        class Region:
            def __init__(self, start=0):
                self.at = start

            def take(self, cols):
                a = self.at
                self.at += cols
                assert self.at <= ARENA, self.at
                return arena[:, a:a + cols]

            def tiles(self, k, n=T):
                return self.take(k * n).rearrange("p (k t) -> p k t", t=n)

        first, split_before = {}, {}
        n0 = n1 = 0
        for name, slots, cols in STREAM:
            first[name], split_before[name] = n0, n1
            n0 += slots
            n1 += slots if name in SPLIT else 0
        slots_of = {name: slots for name, slots, _ in STREAM}
        cols_of = {name: cols for name, _, cols in STREAM}

        def used(name, n):
            return n + (first[name] + RING)

        phase = {"n": {}}
        phase_total = 21

        def barrier(eng, who):
            n = phase["n"].get(who, 0) + 1
            phase["n"][who] = n
            eng.drain().then_inc(sem["phase_end"], 1)
            eng.wait_ge(sem["phase_end"], 4 * n)

        def update_of(d, n):
            bank = ([0, 1, 6, 7] if d == 0 else [2, 3, 4, 5])[n // 4 * 2 + n % 2]
            return ps[:, bank, n // 2 % 2 * GLA_DV:(n // 2 % 2 + 1) * GLA_DV]

        norms = {"act": 0, "pe": 0, "dve": 0, "act_split": 0}
        splits = {"pe": 0, "dve": 0}

        def norm_act(act, src_flat, sq_flat, meanwhile=None):
            n = norms["act"]
            norms["act"] += 1
            for k in range(DT):
                cols = slice(k * T, (k + 1) * T)
                nc.scalar.activation(sq_flat[:, cols], src_flat[:, cols], ACT.Square).then_inc(sem["squares_ready"], 1)
            if meanwhile:
                meanwhile()
            act.wait_ge(sem["sumsq_ready"], n + 1)
            nc.scalar.activation(root[:, :], ps[:, 7, :], ACT.Sqrt, bias=eps, scale=1.0 / D).then_inc(sem["root_ready"], 1)

        def norm_pe(pe, sq):
            n = norms["pe"]
            norms["pe"] += 1
            for k in range(DT):
                pe.wait_ge(sem["squares_ready"], DT * n + k + 1)
                last = nc.tensor.matmul(ps[:, 7, :], ones, sq[:, k, :], start=(k == 0), stop=(k == DT - 1))
            last.then_inc(sem["sumsq_ready"], 1)

        def norm_dve(dve, src, gain, dst):
            n = norms["dve"]
            norms["dve"] += 1
            dve.wait_ge(sem["root_ready"], n + 1)
            nc.vector.reciprocal(rinv[:, :], root[:, :])
            dve.drain()
            for k in range(DT):
                nc.vector.scalar_tensor_tensor(dst[:, k, :], src[:, k, :], con(gain)[:, k:k + 1], rinv[:, :],
                                               ALU.mult, ALU.mult)

        def high_tiles_act(act, src, parts, scaled=False):
            for k in range(DT * len(parts)):
                if scaled:
                    act.wait_ge(sem["hn_scaled"], norms["act_split"] * DT + k + 1)
                nc.scalar.activation(parts[k // DT][0][:, k % DT, :], src[:, k, :], ACT.Copy).then_inc(sem["hn_high"], 1)
            norms["act_split"] += scaled

        def low_tile_dve(dve, src, parts, k, n):
            hi, lo = parts[k // DT]
            dve.wait_ge(sem["hn_high"], n + k + 1)
            nc.vector.tensor_tensor(lo[:, k % DT, :], src[:, k, :], hi[:, k % DT, :].bitcast(F32), ALU.subtract)\
                .then_inc(sem["hn_ready"], 1)

        def low_tiles_dve(dve, src, parts):
            n = splits["dve"]
            splits["dve"] += DT * len(parts)
            for k in range(DT * len(parts)):
                low_tile_dve(dve, src, parts, k, n)

        def norm_split_dve(dve, gain, tmp, lo):
            n = norms["dve"]
            norms["dve"] += 1
            n0 = splits["dve"]
            splits["dve"] += DT
            dve.wait_ge(sem["root_ready"], n + 1)
            nc.vector.reciprocal(rinv[:, :], root[:, :])
            dve.drain()
            for k in range(DT):
                nc.vector.scalar_tensor_tensor(tmp[:, k, :], res[:, k, :], con(gain)[:, k:k + 1], rinv[:, :],
                                               ALU.mult, ALU.mult).then_inc(sem["hn_scaled"], 1)
                if k > 0:
                    low_tile_dve(dve, tmp, [(hn_hi, lo)], k - 1, n0)
            dve.drain()
            low_tile_dve(dve, tmp, [(hn_hi, lo)], DT - 1, n0)

        def over_groups(eng, name, body):
            groups = slots_of[name] // RING
            if groups <= 2:
                for i in range(groups - 1):
                    body(i, False)
            else:
                with eng.Fori(0, groups - 1) as i:
                    body(i, False)
            body(groups - 1, True)

        def next_slot(names, name, i, j, last):
            if j < 2:
                return name, i, j + 2
            if not last:
                return name, i + 1, j - 2
            after = names.index(name) + 1
            return (names[after], 0, j - 2) if after < len(names) else None

        def high_act(act, name, i, j):
            cols = cols_of[name]
            act.wait_ge(landed[j], 16 * i + 16 * (first[name] // RING + 1))
            w_hi, _ = rings(name)
            nc.scalar.activation(w_hi[:, j % 2, 0:cols], ring[:, j, 0:cols], ACT.Copy).then_inc(sem["high_ready"], 1)

        def low_pool(pool, name, i, j):
            cols = cols_of[name]
            pool.wait_ge(sem["high_ready"], RING * i + (split_before[name] + j + 1))
            w_hi, w_lo = rings(name)
            nc.gpsimd.tensor_tensor(w_lo[:, j % 2, 0:cols], ring[:, j, 0:cols], w_hi[:, j % 2, 0:cols].bitcast(F32),
                                    ALU.subtract).then_inc(sem["low_ready"], 1)

        def lows_pool(pool, names):
            for j in range(2):
                low_pool(pool, names[0], 0, j)
            for name in names:
                def group(i, last):
                    for j in range(RING):
                        ahead = next_slot(names, name, i, j, last)
                        if ahead:
                            low_pool(pool, *ahead)
                over_groups(pool, name, group)

        def split_product(name, out_bank, j, kt, x_hi, x_lo, wait_tile=None, start=True, stop=True):
            w_hi, w_lo = rings(name)
            for k in range(kt):
                if wait_tile is not None:
                    wait_tile(k)
                w = slice(k * P, (k + 1) * P)
                nc.tensor.matmul(out_bank, w_hi[:, j % 2, w], x_hi[:, k, :], start=(start and k == 0), stop=False)
                nc.tensor.matmul(out_bank, w_hi[:, j % 2, w], x_lo[:, k, :], start=False, stop=False)
                mm = nc.tensor.matmul(out_bank, w_lo[:, j % 2, w], x_hi[:, k, :], start=False,
                                      stop=(stop and k == kt - 1))
            mm.then_inc(sem["slots_used"], 1)

        def tiles_ready(pe, n):
            before = splits["pe"]
            splits["pe"] += n
            return lambda k: pe.wait_ge(sem["hn_ready"], before + k + 1)

        def project_pe(pe, name, parts, free, tile_ready=None):
            n_parts = len(parts)

            def group(i, last):
                for j in range(RING):
                    t, part = j // n_parts, j % n_parts
                    if part == 0:
                        pe.wait_ge(sem[free[0]], (RING // n_parts) * i + (free[1] + t + 1))
                    pe.wait_ge(sem["low_ready"], RING * i + (split_before[name] + j + 1))
                    split_product(name, ps[:, t, :], j, DT, *parts[part],
                                  wait_tile=(lambda k: tile_ready(DT * part + k)) if tile_ready and t == 0 else None,
                                  start=(part == 0), stop=(part == n_parts - 1))
            over_groups(pe, name, group)

        def project_v_pe(pe, name, copied, x_hi, x_lo):
            for g in range(slots_of[name] // RING):
                if g > 0:
                    pe.wait_ge(sem["v_copied"], copied + TT * g)
                for j in range(RING):
                    pe.wait_ge(sem["low_ready"], split_before[name] + RING * g + j + 1)
                    for k2 in range(2):
                        k = 2 * j + k2
                        w = slice(k2 * 512, (k2 + 1) * 512)
                        for t in range(TT):
                            tok = slice(t * P, (t + 1) * P)
                            o = ps[:, 4 + t, :]
                            nc.tensor.matmul(o, x_hi[:, k, tok], w_hi8[:, j % 2, w], start=(k == 0), stop=False)
                            nc.tensor.matmul(o, x_hi[:, k, tok], w_lo8[:, j % 2, w], start=False, stop=False)
                            mm = nc.tensor.matmul(o, x_lo[:, k, tok], w_hi8[:, j % 2, w], start=False, stop=(k == DT - 1))
                    mm.then_inc(sem["slots_used"], 1)

        def first_highs_act(act, name):
            for j in range(2):
                high_act(act, name, 0, j)

        def project_act(act, names, move=None):
            for name in names:
                def group(i, last):
                    for j in range(RING):
                        act.wait_ge(sem["slots_used"], used(name, RING * i + (j + 1)))
                        ahead = next_slot(names, name, i, j, last)
                        if ahead:
                            high_act(act, *ahead)
                        if move:
                            move(name, i, j)
                over_groups(act, name, group)

        def move_tile(dst, i, j, func=ACT.Copy, scale=1.0):
            nc.scalar.activation(dst[:, RING * i + j, :], ps[:, j, :], func, scale=scale).then_inc(sem["proj_copied"], 1)

        def move_v(dst, i, j):
            if j == RING - 1:
                for t in range(TT):
                    nc.scalar.activation(dst[:, t, i * 512:(i + 1) * 512], ps[:, 4 + t, :], ACT.Copy)\
                        .then_inc(sem["v_copied"], 1)

        ARENA_AT = place["arena"]
        hn_hi = tiled("hn_hi", DT, T, place["hn"], F32R)
        hn_lo = tiled("hn_lo", DT, T, ARENA_AT + ARENA - 8 * D, F32R)
        w_hi8 = tiled("w_hi8", 2, D, ARENA_AT + ARENA - 4 * D, F32R)
        w_lo8 = tiled("w_lo8", 2, D, ARENA_AT + ARENA - 2 * D, F32R)
        mix_hi = tiled("mix_hi", DT, T, ARENA_AT + DT * T, F32R)
        y_hi = tiled("y_hi", DT, T, ARENA_AT + 24 * T, F32R)
        y_lo = tiled("y_lo", DT, T, ARENA_AT + 32 * T, F32R)

        def rings(name):
            return (w_hi, w_lo) if name.startswith("ffn") else (w_hi8, w_lo8)

        r = Region()
        y_even = r.tiles(16)
        ytmp = r.tiles(DT)
        ytmp_flat = ytmp.rearrange("p k t -> p (k t)")
        r = Region(16 * T)
        gw = r.tiles(2, GATE_COLS)
        xa_pad, xb_s, gc_s, gb_s, szb, sza, ua = (r.tiles(2, n) for n in (516, T, T, T, T, T, T))
        u_pad = r.take(516)
        cv = ring[:, 0, 8 * P:8 * P + T]
        rg, ig, ag, tg, hg = (r.tiles(2) for _ in range(5))
        nsp = r.take(16)
        nsp_c = r.tiles(2, 2)
        lt = r.tiles(6, 16)
        assert r.at <= ARENA - 8 * D
        even_tmp = y_even[:, 0:DT, :]

        r = Region()
        qk_o = r.tiles(8)
        r_o = r.tiles(8)
        v_o = r.tiles(TT, GLA_HEADS * GLA_DV)
        lr_t = r.take(T)
        odd_tmp = v_o.rearrange("p t (a b) -> p (t a) b", b=T)
        wz = r.tiles(2, P)
        bz = r.take(2)
        vh = r.tiles(TT, GLA_DV)
        bc, e_p, e_n, kstn, st = (r.tiles(2) for _ in range(5))
        q_in, k_in, k_st = (r.tiles(4) for _ in range(3))
        e_d = r.take(4 * GLA_NCH).rearrange("p (b n) -> p b n", n=GLA_NCH)
        states = r.take(2 * GLA_NCH * GLA_DV).rearrange("p (d n e) -> p d n e", d=2, e=GLA_DV)
        on_o = r.tiles(TT, GLA_DV)
        ssum, sroot, sinv = r.take(TT), r.take(TT), r.take(TT)
        ytmp_o, ytmp_o_flat = qk_o, qk_o.rearrange("p k t -> p (k t)")

        r = Region()
        k_sw = r.tiles(8)
        v_sw = r.tiles(TT, 512)
        k_c = r.take(KV_HEADS * N_CMP)
        v_c = r.take(KV_HEADS * HD)
        KEPT = (r.at + 7) // 8 * 8

        r = Region(KEPT)
        ff = place["arena"] + r.at
        silu_a = r.tiles(2)
        ff_tmp = r.tiles(DT)
        hid_hi = tiled("hid_hi", HALVES[0], T, ff + 2 * T, F32R)
        hid_lo = tiled("hid_lo", HALVES[0], T, ff + (2 + HALVES[0]) * T, F32R)
        rest = ff + (2 + 2 * HALVES[0]) * T
        ff_lo = tiled("ff_lo", DT, T, rest, F32R)
        w_hi = tiled("w_hi", 2, SLOT, rest + DT * T, F32R)
        w_lo = tiled("w_lo", 2, SLOT, rest + DT * T + 2 * SLOT, F32R)
        assert rest + DT * T + 4 * SLOT <= end[0]
        ff_tmp_flat = ff_tmp.rearrange("p k t -> p (k t)")

        r = Region()
        qk_s = r.tiles(16)
        v_s = r.tiles(TT, D)
        CUT = [0, 512, 896, 1152, 1280]
        q_st, k_st_s = r.tiles(2), r.tiles(2)
        v_st = r.take(2 * TT * P).rearrange("p (b k d) -> p b k d", b=2, d=P)
        lg, sp_b, wb = r.tiles(2, 1280), r.tiles(2, 1280), r.tiles(2, 1280)
        SB_AT = [(0, 0), (1, 0), (2, 0), (1, 384)]
        r.at = (r.at + 7) // 8 * 8
        sp_hi = tiled("sp_hi", 2, 1280, ARENA_AT + r.at, F32R)
        sp_lo = tiled("sp_lo", 2, 1280, ARENA_AT + r.at + 2 * 1280, F32R)
        neg_tri_r, neg_ones_r = (at(name, P, ARENA_AT + r.at + (4 * 1280 + n * P), F32R)
                                 for n, name in enumerate(("neg_tri_r", "neg_ones_r")))
        assert r.at + 4 * 1280 + 2 * P <= ARENA

        r = Region(KEPT)
        kt8 = r.tiles(8)
        hr_sq, hr_xn, hr_t1, hr_t2 = (r.take(T) for _ in range(4))
        x2 = r.take(2 * 4 * T).rearrange("p (c g t) -> p c g t", c=2, t=T)
        xb = r.take(2 * 16 * 124).rearrange("p (c m n) -> p c m n", c=2, n=124)
        hid_c = r.take(4 * 124).rearrange("p (c m n) -> p c m n", c=2, n=124)
        kc_raw = r.take(124)

        r = Region(KEPT)
        q_h = r.tiles(16)
        o_n = r.tiles(TT, D)
        q_t = o_n.rearrange("p t (a b) -> p (t a) b", b=T)
        nsa_tmp = q_h[:, 0:DT, :]
        r = Region(r.at)
        hr2_sq, hr2_root = r.tiles(2), r.tiles(2)
        hr2_xn, hr2_t1, hr2_t2 = (r.take(T) for _ in range(3))
        r = Region(KEPT + 16 * T + TT * D)
        pr, prt = r.tiles(2, 1280), r.tiles(2, 1280)
        q_s2 = r.tiles(2)
        zraw, zmax, psm, coef = r.tiles(2, 4), r.tiles(2, 4), r.tiles(3, 4), r.tiles(2, 4)
        gts = r.tiles(TT, 48)
        k_c3 = k_c.rearrange("p (g n) -> p g n", n=N_CMP)
        v_c3 = v_c.rearrange("p (g d) -> p g d", d=HD)
        v_sw4 = v_sw.rearrange("p t (b d) -> p t b d", d=HD)
        NSA_AT = [(1, 384), (2, 0), (1, 0), (0, 0)]
        o_n4 = o_n.rearrange("p t (h d) -> p t h d", d=HD)
        gts_g = gts.rearrange("p t g -> p g t")

        block = ctx.enter_context(nc.Block())

        @block.sync
        def _(sp):
            sp.dma_start(consts[:, :], consts_in).then_inc(sem["const_landed"], 16)
            sp.dma_start(res[:, :, :], x_in).then_inc(sem["x_landed"], 16)
            for name, slots, cols in STREAM:
                if name == "even_in":
                    with sp.Fori(0, RG_HEADS // 2) as i:
                        for jj in range(2):
                            sp.wait_ge(sem["even_channel_done"], 2 * i + (jj + 1))
                            sp.dma_start(gw[:, jj, :], gates_in[2 * i + jj]).then_inc(gate_landed[jj], 16)
                            for n in range(6):
                                s = 6 * jj + n
                                sp.wait_ge(sem["slots_used"], 12 * i + (s + 1))
                                sp.dma_start(ring[:, s % RING, 0:cols], weights[name][12 * i + s])\
                                    .then_inc(landed[s % RING], 16)
                    continue
                with sp.Fori(0, slots // RING) as i:
                    for j in range(RING):
                        sp.wait_ge(sem["slots_used"], RING * i + (first[name] + j + 1))
                        sp.dma_start(ring[:, j, 0:cols], weights[name][RING * i + j]).then_inc(landed[j], 16)
            sp.wait_ge(sem["phase_end"], 4 * phase_total)
            sp.dma_start(out, res[:, :, :]).then_inc(sem["out_stored"], 16)
            sp.wait_ge(sem["out_stored"], 16)

        @block.tensor
        def _(pe):
            B = lambda: barrier(pe, "pe")
            pe.sem_inc(sem["slots_used"], RING)
            pe.sem_inc(sem["o_done"], 1)
            pe.sem_inc(sem["z_done"], 4)
            pe.sem_inc(sem["z2_done"], 6)
            pe.wait_ge(sem["const_landed"], 16)

            norm_pe(pe, even_tmp)
            tile_ready = tiles_ready(pe, DT)
            with pe.Fori(0, RG_HEADS // 2) as i:
                for jj in range(2):
                    for n in range(6):
                        s = 6 * jj + n
                        j = s % RING
                        pe.wait_ge(sem["even_moved"], 12 * i + (s + 1))
                        pe.wait_ge(sem["low_ready"], 12 * i + (s + 1))
                        split_product("even_in", ps[:, j, :], j, DT, hn_hi, hn_lo, tile_ready if s == 0 else None)
                    pe.wait_ge(sem["ua_ready"], 2 * i + (jj + 1))
                    pe.wait_ge(sem["gates_read"], 2 * i + (jj + 1))
                    pe.wait_ge(gate_landed[jj], 16 * i + 16)
                    for g in range(4):
                        mm = nc.tensor.matmul(ps[:, 4 + g, :], gw[:, jj, g * P:(g + 1) * P], ua[:, jj, :],
                                              start=True, stop=True)
                    mm.then_inc(sem["gates_done"], 1)
            B()
            project_pe(pe, "even_out", [(hn_hi, hn_lo), (y_hi, y_lo)], ("even_out_copied", 0), tiles_ready(pe, 2 * DT))
            B()
            norm_pe(pe, hn)
            B()

            norm_pe(pe, odd_tmp)
            project_pe(pe, "odd_qk", [(hn_hi, hn_lo)], ("proj_copied", 0), tiles_ready(pe, DT))
            project_pe(pe, "odd_r", [(hn_hi, hn_lo)], ("proj_copied", 8))
            for k in range(DT):
                mm = nc.tensor.matmul(ps[0:32, 7, :], con("w_lr")[:, k * 32:(k + 1) * 32], odd_tmp[:, k, :],
                                      start=(k == 0), stop=(k == DT - 1))
            mm.then_inc(sem["lr_done"], 1)
            pe.wait_ge(sem["lr_copied"], 1)
            project_v_pe(pe, "odd_v", 0, hn_hi, hn_lo)
            B()
            def gla_gates(h):
                pe.wait_ge(sem["gate_inputs"], h + 1)
                for d in range(2):
                    mm = nc.tensor.matmul(ps[:, d, :], wz[0:32, d, :], lr_t[0:32, :], start=True, stop=True)
                mm.then_inc(sem["gate_done"], 1)

            def gla_head(h, b):
                gla_gates(h + 1)
                pe.wait_ge(sem["o_stored"], h + 1)
                pe.wait_ge(sem["qk_scaled"], h + 2)
                for d in range(2):
                    for t in range(TT):
                        c = slice(t * P, (t + 1) * P)
                        nc.tensor.matmul(ps[:, 2 + d, c], k_in[:, 2 * b + d, c], q_in[:, 2 * b + d, c],
                                         start=True, stop=True)
                        mm = nc.tensor.transpose(ps[:, 4 + d, c], k_st[:, 2 * b + d, c], ident)
                mm.then_inc(sem["scores_done"], 1)
                pe.wait_ge(sem["kst_copied"], h + 1)
                pe.wait_ge(sem["scores_masked"], h + 1)
                pe.wait_ge(sem["gate_read"], h + 2)
                pe.wait_ge(sem["v_ready"], h + 1)
                for d in range(2):
                    for n in range(GLA_NCH):
                        if n == (GLA_NCH - 1 if d == 0 else 0):
                            continue
                        lo = GLA_CHUNK * (n % 2)
                        rows = slice(lo, lo + GLA_CHUNK)
                        mm = nc.tensor.matmul(update_of(d, n),
                                              kstn[rows, d, (n // 2) * P:(n // 2 + 1) * P], vh[rows, n // 2, :],
                                              start=True, stop=True)
                mm.then_inc(sem["updates_done"], 1)
                pe.wait_ge(sem["states_ready"], h + 1)
                for t in range(TT):
                    c = slice(t * P, (t + 1) * P)
                    for d in range(2):
                        nc.tensor.matmul(ps[:, t, 0:GLA_DV], st[:, d, c], vh[:, t, :], start=(d == 0), stop=False,
                                         skip_group_check=True)
                    for half in range(2):
                        n = 2 * t + half
                        for d in range(2):
                            if n == (0 if d == 0 else GLA_NCH - 1):
                                continue
                            mm = nc.tensor.matmul(ps[GLA_CHUNK * half:GLA_CHUNK * (half + 1), t, 0:GLA_DV],
                                                  q_in[:, 2 * b + d, n * GLA_CHUNK:(n + 1) * GLA_CHUNK],
                                                  states[:, d, n, :], start=False, stop=True, skip_group_check=True)
                mm.then_inc(sem["o_done"], 1)
                pe.wait_ge(sem["o_scaled"], h + 1)
                for e in range(2):
                    for t in range(TT):
                        mm = nc.tensor.transpose(ps[:, 4 + e, t * P:(t + 1) * P], on_o[:, t, e * P:(e + 1) * P], ident)
                mm.then_inc(sem["o_turned"], 1)

            gla_gates(0)
            with pe.Fori(0, GLA_HEADS // 2) as i:
                for b in range(2):
                    gla_head(2 * i + b, b)
            B()
            project_pe(pe, "odd_out", [(mix_hi, hn_lo)], ("proj_copied", 16), tiles_ready(pe, DT))
            B()
            norm_pe(pe, hn)
            B()

            def ffn_pe(which, layer, nth):
                norm_pe(pe, ff_tmp)
                tile_ready = tiles_ready(pe, DT)
                for half, n in enumerate(HALVES):
                    before = FT * nth + HALVES[0] * half
                    name = f"{which}_in_{layer}_{half}"

                    def way_in(i, last):
                        for j in range(RING):
                            if j % 2 == 0:
                                pe.wait_ge(sem["hidden_ready"], 2 * i + (before + j // 2 + 1))
                            pe.wait_ge(sem["low_ready"], RING * i + (split_before[name] + j + 1))
                            split_product(name, ps[:, j, :], j, DT, hn_hi, ff_lo,
                                          tile_ready if half == j == 0
                                          else None)
                    over_groups(pe, name, way_in)
                    name_out = f"{which}_out_{layer}_{half}"

                    def way_out(i, last):
                        for j in range(RING):
                            pe.wait_ge(sem["down_done"], RING * i + (2 * DT * nth + DT * half + j + 1))
                            pe.wait_ge(sem["low_ready"], RING * i + (split_before[name_out] + j + 1))
                            split_product(name_out, ps[:, 4 + j, :], j, n, hid_hi, hid_lo,
                                          (lambda k: pe.wait_ge(sem["hidden_ready"], before + k + 3)) if j == 0 else None)
                    over_groups(pe, name_out, way_out)
                B()

            ffn_pe("ffn1", 0, 0)

            norm_pe(pe, qk_s)
            project_pe(pe, "sb_q", [(hn_hi, hn_lo)], ("proj_copied", 24), tiles_ready(pe, DT))
            project_pe(pe, "sb_k", [(hn_hi, hn_lo)], ("proj_copied", 32))
            project_v_pe(pe, "sb_v", 8, hn_hi, hn_lo)
            B()
            def sb_scores(unit, u, i):
                pair, e, bank = u // 2 % 2, u % 2, 3 * (u % 2)
                rows = slice(64 * e, 64 * e + 64)
                if e == 0:
                    pe.wait_ge(sem["sb_copies"], 2 * i + (u // 2 + 1))
                pe.wait_ge(sem["w_done"], unit + 1)
                for t in range(TT):
                    b, at = SB_AT[t]
                    mm = nc.tensor.matmul(ps[:, bank + b, at:at + T - t * P], k_st_s[rows, pair, t * P:(t + 1) * P],
                                          q_st[rows, pair, t * P:T], start=(t < 3), stop=True, skip_group_check=True)
                mm.then_inc(sem["z_done"], 1)

            sb_scores(0, 0, 0)
            pe.wait_ge(sem["sums_ready"], 1)
            with pe.Fori(0, SB_PAIRS // 2) as i:
                def later(u):
                    bank = 3 * (u % 2)
                    pe.wait_ge(sem["sp_ready"], 4 * i + (u + 1))
                    for t in range(TT):
                        b, at = SB_AT[t]
                        for part in (sp_hi, sp_lo):
                            nc.tensor.matmul(ps[:, bank + b, at:at + T - t * P], neg_tri_r[:, :],
                                             part[:, u % 2, CUT[t]:CUT[t + 1]],
                                             start=False, stop=False, skip_group_check=True)
                            for t2 in range(t + 1, TT):
                                col = at + (t2 - t) * P
                                nc.tensor.matmul(ps[:, bank + b, col:col + T - t2 * P], neg_ones_r[:, :],
                                                 part[:, u % 2, CUT[t2]:CUT[t2 + 1]],
                                                 start=False, stop=False, skip_group_check=True)
                        mm = nc.tensor.matmul(ps[:, bank + b, at:at + P], ident_1, sb_neg_1,
                                              start=False, stop=True, skip_group_check=True)
                    mm.then_inc(sem["later_done"], 1)

                def attend(u):
                    pair, e = u // 2, u % 2
                    pe.wait_ge(sem["sb_stored"], 4 * i + (u + 2))
                    if e == 0:
                        pe.wait_ge(sem["sb_values"], 2 * i + (pair + 1))
                    if u == 3:
                        pe.wait_ge(sem["w_done"], 4 * i + (u + 3))
                    for t in range(TT):
                        mm = nc.tensor.matmul(ps[64 * e:64 * e + 64, 6 + e, t * P:T], v_st[:, pair, t, 64 * e:64 * e + 64],
                                              wb[:, e, CUT[t]:CUT[t + 1]], start=(t == 0), stop=(t == TT - 1))
                    mm.then_inc(sem["pv_done"], 1)

                for u in range(4):
                    sb_scores(4 * i + (u + 1), u + 1, i)
                    later(u)
                    if u > 0:
                        attend(u - 1)
                attend(3)
            B()
            project_pe(pe, "sb_out", [(mix_hi, hn_lo)], ("res_added", 0), tiles_ready(pe, DT))
            B()

            ffn_pe("ffn2", 0, 1)

            norm_pe(pe, kt8)
            project_pe(pe, "kv_t", [(hn_hi, hn_lo)], ("proj_copied", 40), tiles_ready(pe, DT))
            project_v_pe(pe, "kv_v", 16, hn_hi, hn_lo)
            B()
            pe.wait_ge(sem["xb_ready"], 1)
            for c in range(2):
                for m in range(16):
                    j = m // 4
                    pe.wait_ge(landed[j], 16 * (first["cmp_w1"] // RING + 1 + c))
                    for mt in range(2):
                        at = ((m % 4) * 2 + mt) * P
                        mm = nc.tensor.matmul(ps[:, 2 * c + mt, 0:124], ring[:, j, at:at + P], xb[:, c, m, :],
                                              start=(m == 0), stop=(m == 15), skip_group_check=True)
                    if m % 4 == 3:
                        mm.then_inc(sem["slots_used"], 1)
            pe.wait_ge(sem["cmp_silu"], 4)
            for mt in range(2):
                mm = nc.tensor.matmul(ps[0:64, 4, 0:124], con("w2_k")[:, mt * 64:(mt + 1) * 64], hid_c[:, 0, mt, :],
                                      start=(mt == 0), stop=(mt == 1))
            for g in range(KV_HEADS):
                for mt in range(2):
                    mm = nc.tensor.matmul(ps[0:N_CMP, 5, g * HD:(g + 1) * HD],
                                          hid_c[:, 1, mt, g * N_CMP:(g + 1) * N_CMP],
                                          con("w2_v")[:, mt * 64:(mt + 1) * 64], start=(mt == 0), stop=(mt == 1))
            mm.then_inc(sem["cmp_out"], 1)

            def head_pe(sq, xn, rows, cols, n):
                pe.wait_ge(sem["hr_squares"], n + 1)
                nc.tensor.matmul(ps[0:rows, 0, 0:cols], con("halves")[0:rows, 0:rows], sq[0:rows, 0:cols],
                                 start=True, stop=True).then_inc(sem["hr_sums"], 1)
                pe.wait_ge(sem["hr_normed"], n + 2)
                nc.tensor.matmul(ps[0:rows, 1, 0:cols], con("rot")[0:rows, 0:rows], xn[0:rows, 0:cols],
                                 start=True, stop=True).then_inc(sem["hr_rotated"], 1)

            head_pe(hr_sq, hr_xn, 64, 124, 0)
            for m in range(4):
                head_pe(hr_sq, hr_xn, P, T, 1 + m)
            B()

            ffn_pe("ffn1", 1, 2)

            norm_pe(pe, nsa_tmp)
            project_pe(pe, "nsa_q", [(hn_hi, hn_lo)], ("proj_copied", 48), tiles_ready(pe, DT))
            for t in range(TT):
                for k in range(DT):
                    mm = nc.tensor.matmul(ps[:, 6, t * 48:(t + 1) * 48], nsa_tmp[:, k, t * P:(t + 1) * P],
                                          con("w_gates")[:, k * 48:(k + 1) * 48], start=(k == 0), stop=(k == DT - 1))
            mm.then_inc(sem["gates_mm"], 1)
            B()
            def q_sums(m, b):
                pe.wait_ge(sem["hr_squares"], m + 6)
                nc.tensor.matmul(ps[:, 2 * b, :], con("halves"), hr2_sq[:, b, :], start=True, stop=True)\
                    .then_inc(sem["hr_sums"], 1)

            q_sums(0, 0)
            with pe.Fori(0, DT // 2) as i:
                for b in range(2):
                    q_sums(2 * i + (b + 1), 1 - b)
                    pe.wait_ge(sem["hr_normed"], 2 * i + (b + 7))
                    nc.tensor.matmul(ps[:, 1, :], con("rot"), hr2_xn[:, :], start=True, stop=True)\
                        .then_inc(sem["hr_rotated"], 1)
            B()
            pe.wait_ge(sem["q_static"], 1)
            for t in range(TT):
                b, at = NSA_AT[t]
                nc.tensor.matmul(ps[:, b, at:at + (t + 1) * P], q_s2[0:64, 0, t * P:(t + 1) * P],
                                 k_sw[0:64, 0, 0:(t + 1) * P], start=True, stop=False)
                mm = nc.tensor.matmul(ps[:, b, at + t * P:at + (t + 1) * P], ident_1, causal_1, start=False, stop=True)
            mm.then_inc(sem["z2_done"], 1)
            with pe.Fori(0, SB_PAIRS) as p:
                def z_mm(u):
                    e, br, bank = u // 3 % 2, u % 3, 3 * (u % 2)
                    group = p // 2 if u < 6 else (p + 1) % SB_PAIRS // 2
                    if br == 0:
                        pe.wait_ge(sem["q_static"], 2 * p + (u // 3 + 1))
                    pe.wait_ge(sem["first_turned"], 6 * p + (u + 1))
                    pe.wait_ge(sem["rest_turned"], 6 * p + (u + 1))
                    for t in range(TT):
                        q = q_s2[0:64, e, t * P:(t + 1) * P]
                        if br < 2:
                            b, at = NSA_AT[t]
                            whole, own = ps[:, bank + b, at:at + (t + 1) * P], ps[:, bank + b, at + t * P:at + (t + 1) * P]
                            mask, keys = causal_1, k_sw[0:64, group + 4 * br, 0:(t + 1) * P]
                        else:
                            whole = own = ps[:, bank + 1, t * N_CMP:(t + 1) * N_CMP]
                            mask, keys = neg_c_1[:, t * N_CMP:(t + 1) * N_CMP], k_c3[0:64, group, :]
                        if t == 0:
                            nc.tensor.matmul(own, ident_1, mask, start=True, stop=False)
                            mm = nc.tensor.matmul(whole, q, keys, start=False, stop=True)
                        else:
                            nc.tensor.matmul(whole, q, keys, start=True, stop=False)
                            mm = nc.tensor.matmul(own, ident_1, mask, start=False, stop=True)
                    mm.then_inc(sem["z2_done"], 1)

                def turn(u):
                    br, b, bank = u % 3, u % 2, 3 * (u % 2)
                    pe.wait_ge(sem["probs_ready"], 6 * p + (u + 1))
                    if br < 2:
                        for t2 in range(TT):
                            tb, at = NSA_AT[TT - 1 - t2]
                            for t in range(t2, TT):
                                off = P * (t * (t + 1) // 2 + t2)
                                col = at + (t - t2) * P
                                mm = nc.tensor.transpose(ps[:, bank + tb, col:col + P], pr[:, b, off:off + P], ident)
                    else:
                        for t in range(TT):
                            half = ps[0:N_CMP, bank + t // 2 * 2, t % 2 * P:(t % 2 + 1) * P]
                            mm = nc.tensor.transpose(half,
                                                     pr[:, b, t * N_CMP:(t + 1) * N_CMP], ident)
                    mm.then_inc(sem["turned"], 1)

                def attend(u):
                    br, b = u % 3, u % 2
                    pe.wait_ge(sem["combined"], 6 * p + (u + 1))
                    if u == 5:
                        pe.wait_ge(sem["first_turned"], 6 * p + (u + 3))
                        pe.wait_ge(sem["rest_turned"], 6 * p + (u + 3))
                    if br == 2:
                        nc.tensor.matmul(ps[:, 6 + b, 0:2], ident_1, ident_1[:, 0:2], start=True, stop=True)
                    for t in range(TT):
                        o = ps[:, 6 + b, t * HD:(t + 1) * HD]
                        if br < 2:
                            for t2 in range(t + 1):
                                at = CUT[t2] + (t - t2) * P
                                mm = nc.tensor.matmul(o, prt[:, b, at:at + P],
                                                      v_sw4[:, t2, p // 2 + 4 * br, :], start=(t2 == 0), stop=(t2 == t))
                        else:
                            mm = nc.tensor.matmul(o, prt[0:N_CMP, b, t * P:(t + 1) * P],
                                                  v_c3[0:N_CMP, p // 2, :], start=True, stop=True)
                    mm.then_inc(sem["attended"], 1)

                for u in range(6):
                    z_mm(u + 1)
                    turn(u)
                    if u > 0:
                        attend(u - 1)
                attend(5)
            B()
            for k in range(DT):
                if k >= 4:
                    pe.wait_ge(sem["mix_copied"], k - 3)
                for t in range(TT):
                    mm = nc.tensor.transpose(ps[:, k % 4, t * P:(t + 1) * P], o_n[:, t, k * P:(k + 1) * P], ident)
                mm.then_inc(sem["mix_turned"], 1)
            B()
            project_pe(pe, "nsa_out", [(mix_hi, hn_lo)], ("res_added", 8), tiles_ready(pe, DT))
            B()
            ffn_pe("ffn2", 1, 3)

        @block.scalar
        def _(act):
            B = lambda: barrier(act, "act")
            act.sem_inc(sem["even_moved"], RING)
            act.sem_inc(sem["gates_read"], 1)
            act.sem_inc(sem["even_out_copied"], 2)
            act.sem_inc(sem["proj_copied"], RING)
            act.sem_inc(sem["w_done"], 2)
            act.sem_inc(sem["rest_turned"], 2)
            act.wait_ge(sem["const_landed"], 16)
            act.wait_ge(sem["x_landed"], 16)
            nc.scalar.activation(lt[:, 0, :], con("lam"), ACT.Abs)
            act.drain()
            nc.scalar.activation(lt[:, 1, :], lt[:, 0, :], ACT.Exp, scale=-1.0)
            even_flat = even_tmp.rearrange("p k t -> p (k t)")
            norm_act(act, res_flat, even_flat, lambda: first_highs_act(act, "even_in"))
            high_tiles_act(act, even_tmp, [(hn_hi, hn_lo)], scaled=True)

            def even_heads(i, last):
                for jj in range(2):
                    act.wait_ge(sem["even_channel_done"], 2 * i + (jj + 1))
                    dsts = [(xa_pad[:, jj, 2:2 + T], ACT.Copy), (xb_s[:, jj, :], ACT.Copy), (gc_s[:, jj, :], ACT.Copy),
                            (gb_s[:, jj, :], ACT.Copy), (szb[:, jj, :], ACT.Silu), (sza[:, jj, :], ACT.Silu)]
                    for n, (dst, func) in enumerate(dsts):
                        s = 6 * jj + n
                        act.wait_ge(sem["slots_used"], 12 * i + (s + 1 + RING))
                        if s < 10 or not last:
                            high_act(act, "even_in", 3 * i + (s + 2) // RING, (s + 2) % RING)
                        nc.scalar.activation(dst, ps[:, s % RING, :], func).then_inc(sem["even_moved"], 1)
                    par = gw[:, jj, 4 * P:4 * P + 16]
                    act.wait_ge(sem["gates_done"], 2 * i + (jj + 1))
                    for d in range(2):
                        nc.scalar.activation(rg[:, d, :], ps[:, 4 + 2 * d, :], ACT.Sigmoid, bias=par[:, 2 * d:2 * d + 1])
                        a = nc.scalar.activation(ig[:, d, :], ps[:, 5 + 2 * d, :], ACT.Sigmoid,
                                                 bias=par[:, 2 * d + 1:2 * d + 2])
                    a.then_inc(sem["gates_read"], 1)
                    act.drain()
                    for d in range(2):
                        nc.scalar.activation(ag[:, d, :], rg[:, d, :], ACT.Exp, scale=nsp_c[:, jj, d:d + 1])
                    for d in range(2):
                        a = nc.scalar.activation(hg[:, d, :], rg[:, d, :], ACT.Tanh, scale=nsp_c[:, jj, d:d + 1])
                    a.then_inc(sem["decay_ready"], 1)
                    for d in range(2):
                        act.wait_ge(sem["factor_ready"], 4 * i + (2 * jj + d + 1))
                        nc.scalar.activation(rg[:, d, :], tg[:, d, :], ACT.Sqrt, scale=-1.0)\
                            .then_inc(sem["root_b_ready"], 1)

            with act.Fori(0, RG_HEADS // 2 - 1) as i:
                even_heads(i, False)
            even_heads(RG_HEADS // 2 - 1, True)
            B()
            first_highs_act(act, "even_out")
            high_tiles_act(act, y_even, [(hn_hi, hn_lo), (y_hi, y_lo)])

            def move_even(name, i, j):
                if j % 2 == 1:
                    nc.scalar.activation(ytmp[:, 2 * i + j // 2, :], ps[:, j // 2, :], ACT.Copy)\
                        .then_inc(sem["even_out_copied"], 1)
            project_act(act, ["even_out"], move_even)
            B()
            norm_act(act, ytmp_flat, hn_flat)
            B()

            norm_act(act, res_flat, odd_tmp.rearrange("p k t -> p (k t)"), lambda: first_highs_act(act, "odd_qk"))
            high_tiles_act(act, odd_tmp, [(hn_hi, hn_lo)], scaled=True)

            def move_odd(name, i, j):
                if name == "odd_v":
                    move_v(v_o, i, j)
                elif name == "odd_qk":
                    move_tile(qk_o, i, j)
                else:
                    move_tile(r_o, i, j, ACT.Silu)
                    if (i, j) == (1, RING - 1):
                        act.wait_ge(sem["lr_done"], 1)
                        nc.scalar.activation(lr_t[0:32, :], ps[0:32, 7, :], ACT.Copy).then_inc(sem["lr_copied"], 1)
            project_act(act, ["odd_qk", "odd_r", "odd_v"], move_odd)
            B()
            def gla_logs(h, b):
                act.preload_act_table_set(LOG_SET)
                act.wait_ge(sem["gate_done"], h + 1)
                act.wait_ge(sem["gate_inputs"], h + 1)
                for d in range(2):
                    a = nc.scalar.activation(q_in[:, 2 * b + d, :], ps[:, d, :], ACT.Identity, bias=bz[:, d:d + 1])
                act.drain().then_inc(sem["gate_read"], 1)
                act.wait_ge(sem["qk_scaled"], h + 1)
                nc.scalar.activation(e_p[:, :, :], q_in[:, 2 * b:2 * b + 2, :], ACT.Abs)
                act.drain()
                nc.scalar.activation(e_p[:, :, :], e_p[:, :, :], ACT.Exp, scale=-1.0)
                act.drain()
                nc.scalar.activation(e_n[:, :, :], e_p[:, :, :], ACT.Ln, bias=1.0).then_inc(sem["gate_log"], 1)

            def gla_exps(h, b):
                act.wait_ge(sem["cum_ready"], h + 1)
                nc.scalar.activation(e_p[:, :, :], bc[:, :, :], ACT.Exp, scale=1.0 / 16)
                nc.scalar.activation(e_n[:, :, :], bc[:, :, :], ACT.Exp, scale=-1.0 / 16)
                k2 = k_st[:, 2 * b:2 * b + 2, :]
                nc.scalar.activation(k2, k2, ACT.Exp, scale=1.0 / 16).then_inc(sem["exps_ready"], 1)

            def gla_head(h, b):
                gla_logs(h + 1, 1 - b)
                act.wait_ge(sem["scores_done"], h + 1)
                for d in range(2):
                    a = nc.scalar.activation(kstn[:, d, :], ps[:, 4 + d, :], ACT.Copy)
                a.then_inc(sem["kst_copied"], 1)
                gla_exps(h + 1, 1 - b)
                act.wait_ge(sem["o_done"], h + 2)
                for t in range(TT):
                    nc.scalar.activation(kstn[:, t % 2, (t // 2) * 256:(t // 2) * 256 + 256], ps[:, t, 0:GLA_DV],
                                         ACT.Square, accum_out=ssum[:, t:t + 1])
                act.drain()
                nc.scalar.activation(sroot, ssum, ACT.Sqrt, bias=eps, scale=1.0 / GLA_DV).then_inc(sem["o_squared"], 1)

            gla_logs(0, 0)
            gla_exps(0, 0)
            with act.Fori(0, GLA_HEADS // 2) as i:
                for b in range(2):
                    gla_head(2 * i + b, b)
            B()
            first_highs_act(act, "odd_out")
            high_tiles_act(act, hn, [(mix_hi, hn_lo)])
            project_act(act, ["odd_out"], lambda name, i, j: move_tile(ytmp_o, i, j))
            B()
            norm_act(act, ytmp_o_flat, hn_flat)
            B()

            def ffn_act(which, layer, nth):
                names = [name for name, _, _ in ffn_stream(which, layer)]
                norm_act(act, res_flat, ff_tmp_flat, lambda: first_highs_act(act, names[0]))
                high_tiles_act(act, ff_tmp, [(hn_hi, ff_lo)], scaled=True)
                for name in names:
                    half = int(name[-1])
                    before = FT * nth + HALVES[0] * half

                    def group(i, last):
                        for j in range(RING):
                            act.wait_ge(sem["slots_used"], used(name, RING * i + (j + 1)))
                            ahead = next_slot(names, name, i, j, last)
                            if ahead:
                                high_act(act, *ahead)
                            if "_in_" in name and j % 2 == 0:
                                act.wait_ge(sem["hidden_ready"], 2 * i + (before + j // 2 + 1))
                                nc.scalar.activation(silu_a[:, j // 2, :], ps[:, j, :], ACT.Silu)\
                                    .then_inc(sem["silu_done"], 1)
                    over_groups(act, name, group)
                B()

            ffn_act("ffn1", 0, 0)

            norm_act(act, res_flat, qk_s[:, 0:DT, :].rearrange("p k t -> p (k t)"), lambda: first_highs_act(act, "sb_q"))
            high_tiles_act(act, qk_s, [(hn_hi, hn_lo)], scaled=True)

            def move_sb(name, i, j):
                if name == "sb_v":
                    move_v(v_s, i, j)
                elif name == "sb_q":
                    move_tile(qk_s, i, j, scale=HD ** -0.5)
                else:
                    move_tile(qk_s[:, DT:2 * DT, :], i, j)
            project_act(act, ["sb_q", "sb_k", "sb_v"], move_sb)
            B()
            act.preload_act_table_set(LOG_SET)
            def logs(unit, u):
                e, bank = u % 2, 3 * (u % 2)
                act.wait_ge(sem["z_done"], unit + 5)
                for t in range(TT):
                    b, at = SB_AT[t]
                    nc.scalar.activation(lg[:, e, CUT[t]:CUT[t + 1]], ps[:, bank + b, at:at + T - t * P], ACT.Abs)
                act.drain()
                nc.scalar.activation(lg[:, e, :], lg[:, e, :], ACT.Exp, scale=-1.0)
                act.drain()
                nc.scalar.activation(lg[:, e, :], lg[:, e, :], ACT.Ln, bias=1.0).then_inc(sem["log_done"], 1)

            logs(0, 0)
            with act.Fori(0, SB_PAIRS // 2) as i:
                for u in range(4):
                    logs(4 * i + (u + 1), u + 1)
                    e, bank = u % 2, 3 * (u % 2)
                    act.wait_ge(sem["later_done"], 4 * i + (u + 1))
                    for t in range(TT):
                        b, at = SB_AT[t]
                        a = nc.scalar.activation(wb[:, e, CUT[t]:CUT[t + 1]], ps[:, bank + b, at:at + T - t * P], ACT.Exp)
                    a.then_inc(sem["w_done"], 1)
            B()
            first_highs_act(act, "sb_out")
            high_tiles_act(act, hn, [(mix_hi, hn_lo)])
            project_act(act, ["sb_out"])
            B()

            ffn_act("ffn2", 0, 1)

            norm_act(act, res_flat, kt8.rearrange("p k t -> p (k t)"), lambda: first_highs_act(act, "kv_t"))
            high_tiles_act(act, kt8, [(hn_hi, hn_lo)], scaled=True)
            project_act(act, ["kv_t", "kv_v"],
                        lambda name, i, j: move_v(v_sw, i, j) if name == "kv_v" else move_tile(kt8, i, j))
            B()
            act.wait_ge(sem["slots_used"], used("cmp_w1", 8))
            for c in range(2):
                for mt in range(2):
                    nc.scalar.activation(hid_c[:, c, mt, :], ps[:, 2 * c + mt, 0:124], ACT.Silu)\
                        .then_inc(sem["cmp_silu"], 1)
            act.wait_ge(sem["cmp_out"], 1)
            nc.scalar.activation(kc_raw[0:64, :], ps[0:64, 4, 0:124], ACT.Copy)
            nc.scalar.activation(v_c[0:N_CMP, :], ps[0:N_CMP, 5, 0:256], ACT.Copy)
            act.drain().then_inc(sem["cmp_copied"], 1)

            def head_act(src, sq, rows, cols, n):
                nc.scalar.activation(sq[0:rows, 0:cols], src, ACT.Square).then_inc(sem["hr_squares"], 1)
                act.wait_ge(sem["hr_sums"], n + 1)
                act.wait_ge(sem["hr_normed"], n + 1)
                nc.scalar.activation(root[0:rows, 0:cols], ps[0:rows, 0, 0:cols], ACT.Sqrt, bias=eps[0:rows, :],
                                     scale=1.0 / HD).then_inc(sem["hr_root"], 1)

            head_act(kc_raw[0:64, :], hr_sq, 64, 124, 0)
            for m in range(4):
                head_act(kt8[:, 4 + m, :], hr_sq, P, T, 1 + m)
            B()

            ffn_act("ffn1", 1, 2)

            norm_act(act, res_flat, nsa_tmp.rearrange("p k t -> p (k t)"), lambda: first_highs_act(act, "nsa_q"))
            high_tiles_act(act, nsa_tmp, [(hn_hi, hn_lo)], scaled=True)
            project_act(act, ["nsa_q"], lambda name, i, j: move_tile(q_t, i, j))
            act.wait_ge(sem["gates_mm"], 1)
            nc.scalar.activation(gts.rearrange("p t g -> p (t g)"), ps[:, 6, 0:192], ACT.Sigmoid)
            B()
            def q_root(m, b, tile):
                nc.scalar.activation(hr2_sq[:, b, :], q_t[:, tile, :], ACT.Square).then_inc(sem["hr_squares"], 1)
                act.wait_ge(sem["hr_sums"], m + 6)
                act.wait_ge(sem["hr_normed"], m + 5)
                nc.scalar.activation(hr2_root[:, b, :], ps[:, 2 * b, :], ACT.Sqrt, bias=eps, scale=1.0 / HD)\
                    .then_inc(sem["hr_root"], 1)

            q_root(0, 0, 0)
            with act.Fori(0, DT // 2) as i:
                for b in range(2):
                    q_root(2 * i + (b + 1), 1 - b, 2 * i + 1 if b == 0 else (i + 1) % (DT // 2) * 2)
            B()
            def probs(unit, u):
                br, b, bank = u % 3, u % 2, 3 * (u % 2)
                act.wait_ge(sem["max_ready"], unit + 1)
                for t in range(TT):
                    if br < 2:
                        off = P * (t * (t + 1) // 2)
                        tb, at = NSA_AT[t]
                        dst, src = pr[:, b, off:off + (t + 1) * P], ps[:, bank + tb, at:at + (t + 1) * P]
                    else:
                        dst, src = pr[:, b, t * N_CMP:(t + 1) * N_CMP], ps[:, bank + 1, t * N_CMP:(t + 1) * N_CMP]
                    nc.scalar.activation(dst, src, ACT.Exp, bias=zmax[:, b, t:t + 1], scale=HD ** -0.5,
                                         accum_out=psm[:, u % 3, t:t + 1])
                act.drain().then_inc(sem["probs_ready"], 1)

            probs(0, 0)
            with act.Fori(0, SB_PAIRS) as p:
                for u in range(6):
                    b, bank = u % 2, 3 * (u % 2)
                    act.wait_ge(sem["turned"], 6 * p + (u + 1))
                    if u % 3 < 2:
                        for t2 in range(1, TT):
                            tb, at = NSA_AT[TT - 1 - t2]
                            a = nc.scalar.activation(prt[:, b, CUT[t2]:CUT[t2 + 1]], ps[:, bank + tb, at:at + T - t2 * P],
                                                     ACT.Copy)
                        a.then_inc(sem["rest_turned"], 1)
                    else:
                        nc.scalar.activation(prt[0:N_CMP, b, 2 * P:T], ps[0:N_CMP, bank + 2, 0:2 * P], ACT.Copy)\
                            .then_inc(sem["rest_turned"], 1)
                    probs(6 * p + (u + 1), u + 1)
            B()
            for k in range(DT):
                act.wait_ge(sem["mix_turned"], k + 1)
                nc.scalar.activation(hn[:, k, :], ps[:, k % 4, :], ACT.Copy).then_inc(sem["mix_copied"], 1)
            B()
            first_highs_act(act, "nsa_out")
            high_tiles_act(act, hn, [(mix_hi, hn_lo)])
            project_act(act, ["nsa_out"])
            B()
            ffn_act("ffn2", 1, 3)

        @block.vector
        def _(dve):
            B = lambda: barrier(dve, "dve")
            V = nc.vector
            dve.sem_inc(sem["even_channel_done"], 2)
            dve.sem_inc(sem["hidden_ready"], 2)
            dve.sem_inc(sem["down_done"], RING)
            dve.sem_inc(sem["res_added"], RING)
            dve.sem_inc(sem["o_stored"], 1)
            dve.sem_inc(sem["qk_scaled"], 1)
            dve.sem_inc(sem["sb_stored"], 3)
            dve.sem_inc(sem["hr_normed"], 1)
            dve.sem_inc(sem["combined"], 2)
            dve.sem_inc(sem["first_turned"], 2)
            dve.wait_ge(sem["const_landed"], 16)
            dve.wait_ge(sem["x_landed"], 16)
            for jj in range(2):
                V.memset(xa_pad[:, jj, 0:2], 0.0)
                V.memset(xa_pad[:, jj, 2 + T:3 + T], 0.0)
            V.memset(u_pad[:, 0:1], 0.0)
            V.memset(u_pad[:, 1 + T:2 + T], 0.0)
            dve.wait_ge(sem["squares_ready"], 1)
            V.tensor_scalar(lt[:, 2, :], lt[:, 1, :], 2.0, None, ALU.add)
            dve.drain()
            V.reciprocal(lt[:, 3, :], lt[:, 2, :])
            dve.drain()
            V.tensor_tensor(lt[:, 2, :], lt[:, 1, :], lt[:, 3, :], ALU.mult)
            dve.drain()
            V.tensor_tensor(lt[:, 3, :], lt[:, 2, :], lt[:, 2, :], ALU.mult)
            V.memset(lt[:, 4, :], 1.0 / 19)
            dve.drain()
            for odd in range(17, -1, -2):
                V.tensor_tensor(lt[:, 5, :], lt[:, 4, :], lt[:, 3, :], ALU.mult)
                dve.drain()
                V.tensor_scalar(lt[:, 4, :], lt[:, 5, :], 1.0 / odd, None, ALU.add)
                dve.drain()
            V.tensor_tensor(lt[:, 5, :], lt[:, 4, :], lt[:, 2, :], ALU.mult)
            V.tensor_scalar(lt[:, 3, :], con("lam"), -1.0, 0.0, ALU.mult, ALU.max)
            dve.drain()
            V.scalar_tensor_tensor(lt[:, 4, :], lt[:, 5, :], 2.0, lt[:, 3, :], ALU.mult, ALU.add)
            dve.drain()
            V.tensor_scalar(nsp, lt[:, 4, :], -8.0, None, ALU.mult)
            norm_split_dve(dve, "g_even_pre", even_tmp, hn_lo)
            nsp2 = nsp.rearrange("p (c d) -> p c d", d=2)
            with dve.Fori(0, RG_HEADS // 2) as i:
                for jj in range(2):
                    par = gw[:, jj, 4 * P:4 * P + 16]
                    dve.wait_ge(gate_landed[jj], 16 * i + 16)
                    V.tensor_copy(nsp_c[:, jj, :], nsp2[:, 2 * i + jj, :])
                    dve.wait_ge(sem["even_moved"], 12 * i + (6 * jj + 1 + RING))
                    V.tensor_scalar(ua[:, jj, :], xa_pad[:, jj, 0:T], par[:, 4:5], par[:, 8:9], ALU.mult, ALU.add)
                    for k in range(1, 4):
                        dve.drain()
                        op = V.scalar_tensor_tensor(ua[:, jj, :], xa_pad[:, jj, k:k + T], par[:, 4 + k:5 + k],
                                                    ua[:, jj, :], ALU.mult, ALU.add)
                    op.then_inc(sem["ua_ready"], 1)
                    dve.wait_ge(sem["even_moved"], 12 * i + (6 * jj + 3 + RING))
                    V.tensor_tensor(u_pad[:, 1:1 + T], gc_s[:, jj, :], xb_s[:, jj, :], ALU.mult)
                    dve.drain()
                    V.tensor_scalar(cv, u_pad[:, 0:T], par[:, 9:10], None, ALU.mult)
                    for k in range(1, 3):
                        dve.drain()
                        V.scalar_tensor_tensor(cv, u_pad[:, k:k + T], par[:, 9 + k:10 + k], cv, ALU.mult, ALU.add)
                    dve.drain()
                    dve.wait_ge(sem["even_moved"], 12 * i + (6 * jj + 6 + RING))
                    V.tensor_tensor(cv, cv, gb_s[:, jj, :], ALU.mult)
                    dve.drain()
                    V.tensor_tensor(y_even[:, 2 * i + (jj + 8), :], cv, szb[:, jj, :], ALU.mult)
                    dve.wait_ge(sem["decay_ready"], 2 * i + (jj + 1))
                    for d in range(2):
                        V.tensor_tensor(tg[:, d, :], ag[:, d, :], ag[:, d, :], ALU.mult)
                        dve.drain()
                        V.scalar_tensor_tensor(tg[:, d, :], tg[:, d, :], 1.0, hg[:, d, :], ALU.add, ALU.mult)\
                            .then_inc(sem["factor_ready"], 1)
                        V.tensor_tensor(ig[:, d, :], ig[:, d, :], ua[:, jj, :], ALU.mult)
                    for d in range(2):
                        dve.drain()
                        dve.wait_ge(sem["root_b_ready"], 4 * i + (2 * jj + d + 1))
                        V.tensor_tensor(tg[:, d, :], ig[:, d, :], rg[:, d, :], ALU.mult)
                        dve.drain()
                        way = slice(None, None, 1 if d == 0 else -1)
                        V.tensor_tensor_scan(hg[:, d, way], ag[:, d, way], tg[:, d, way], 0.0, ALU.mult, ALU.add)
                    dve.drain()
                    V.tensor_tensor(tg[:, 0, :], hg[:, 0, :], hg[:, 1, :], ALU.add)
                    dve.drain()
                    V.tensor_tensor(y_even[:, 2 * i + jj, :], tg[:, 0, :], sza[:, jj, :], ALU.mult)\
                        .then_inc(sem["even_channel_done"], 1)
            B()
            low_tiles_dve(dve, y_even, [(hn_hi, hn_lo), (y_hi, y_lo)])
            B()

            def post_norm(y, y_flat, gain):
                norm_dve(dve, y, gain, y)
                dve.drain()
                V.tensor_tensor(res_flat, res_flat, y_flat, ALU.add)

            post_norm(ytmp, ytmp_flat, "g_even_post")
            B()

            norm_split_dve(dve, "g_odd_pre", odd_tmp, hn_lo)
            V.memset(st[:, :, :], 0.0)
            B()
            gla_keep = con("gla_keep").rearrange("p (d t) -> p d t", d=2).bitcast(U32)
            chunk_keep = con("chunk_keep").rearrange("p (d t) -> p d t", d=2)
            def gla_sums(h, b):
                dve.wait_ge(sem["gate_log"], h + 1)
                la = k_in[:, 2 * b:2 * b + 2, :]
                V.scalar_tensor_tensor(la, q_in[:, 2 * b:2 * b + 2, :], 0.0, e_n[:, :, :], ALU.min, ALU.subtract)
                dve.drain()
                for d in range(2):
                    way = slice(None, None, 1 if d == 0 else -1)
                    V.tensor_tensor_scan(bc[:, d, way], chunk_keep[:, d, way], k_in[:, 2 * b + d, way], 0.0,
                                         ALU.mult, ALU.add)
                dve.drain()
                for d in range(2):
                    b3 = bc[:, d, :].rearrange("p (n t) -> p n t", t=GLA_CHUNK)
                    end = GLA_CHUNK - 1 if d == 0 else 0
                    op = V.tensor_tensor(k_st[:, 2 * b + d, :].rearrange("p (n t) -> p n t", t=GLA_CHUNK),
                                         b3[:, :, end:end + 1].to_broadcast([P, GLA_NCH, GLA_CHUNK]), b3, ALU.subtract)
                op.then_inc(sem["cum_ready"], 1)

            def gla_scale(h, b, head):
                dve.wait_ge(sem["exps_ready"], h + 1)
                for d in range(2):
                    x = 2 * b + d
                    edge = GLA_CHUNK - 1 if d == 0 else 0
                    V.tensor_copy(e_d[:, x, :], e_p[:, d, edge:edge + (GLA_NCH - 1) * GLA_CHUNK + 1:GLA_CHUNK])
                    V.scalar_tensor_tensor(q_in[:, x, :], qk_o[:, head, :], float(GLA_DK) ** -0.5, e_p[:, d, :],
                                           ALU.mult, ALU.mult)
                    V.tensor_tensor(k_in[:, x, :], qk_o[:, head + 4, :], e_n[:, d, :], ALU.mult)
                    op = V.tensor_tensor(k_st[:, x, :], qk_o[:, head + 4, :], k_st[:, x, :], ALU.mult)
                op.then_inc(sem["qk_scaled"], 1)
                dve.drain()

            def gla_head(i, b):
                h = 2 * i + b
                dve.wait_ge(sem["scores_done"], h + 1)
                V.memset(sinv, 0.0)
                for d in range(2):
                    op = V.copy_predicated(st[:, d, :], gla_keep[:, d, :], ps[:, 2 + d, :])
                op.then_inc(sem["scores_masked"], 1)
                gla_sums(h + 1, 1 - b)
                dve.wait_ge(sem["updates_done"], h + 1)
                for step in range(GLA_NCH - 1):
                    if step > 0:
                        dve.drain()
                    for d in range(2):
                        n = step if d == 0 else GLA_NCH - 1 - step
                        nxt = n + (1 if d == 0 else -1)
                        upd = update_of(d, n)
                        if step == 0:
                            op = V.tensor_copy(states[:, d, nxt, :], upd)
                        else:
                            op = V.scalar_tensor_tensor(states[:, d, nxt, :], states[:, d, n, :],
                                                        e_d[:, 2 * b + d, n:n + 1], upd, ALU.mult, ALU.add)
                op.then_inc(sem["states_ready"], 1)
                gla_scale(h + 1, 1 - b, 2 * i + 1 if b == 0 else (i + 1) % 2 * 2)
                dve.wait_ge(sem["o_squared"], h + 1)
                V.reciprocal(sinv, sroot)
                dve.drain()
                for t in range(TT):
                    op = V.tensor_scalar(on_o[:, t, :], ps[:, t, 0:GLA_DV], sinv[:, t:t + 1], None, ALU.mult)
                op.then_inc(sem["o_scaled"], 1)
                dve.wait_ge(sem["o_turned"], h + 1)
                for e in range(2):
                    op = V.scalar_tensor_tensor(hn[:, 2 * h + e, :], ps[:, 4 + e, :], con("gla_g")[:, e:e + 1],
                                                r_o[:, 2 * h + e, :], ALU.mult, ALU.mult)
                op.then_inc(sem["o_stored"], 1)

            gla_sums(0, 0)
            gla_scale(0, 0, 0)
            with dve.Fori(0, GLA_HEADS // 2) as i:
                for b in range(2):
                    gla_head(i, b)
            B()
            low_tiles_dve(dve, hn, [(mix_hi, hn_lo)])
            B()
            post_norm(ytmp_o, ytmp_o_flat, "g_odd_post")
            B()

            def ffn_dve(which, layer, nth):
                norm_split_dve(dve, f"g_{which}_{layer}", ff_tmp, ff_lo)
                for half, n in enumerate(HALVES):
                    before = FT * nth + HALVES[0] * half
                    name = f"{which}_in_{layer}_{half}"
                    with dve.Fori(0, n // 2) as i:
                        for j in range(2):
                            dve.drain()
                            dve.wait_ge(sem["silu_done"], 2 * i + (before + j + 1))
                            dve.wait_ge(sem["slots_used"], used(name, 4 * i + (2 * j + 2)))
                            V.tensor_tensor(silu_a[:, j, :], silu_a[:, j, :], ps[:, 2 * j + 1, :], ALU.mult)
                            dve.drain()
                            V.tensor_copy(hid_hi[:, 2 * i + j, :], silu_a[:, j, :])
                            dve.drain()
                            V.tensor_tensor(hid_lo[:, 2 * i + j, :], silu_a[:, j, :],
                                            hid_hi[:, 2 * i + j, :].bitcast(F32), ALU.subtract)\
                                .then_inc(sem["hidden_ready"], 1)
                    name_out = f"{which}_out_{layer}_{half}"
                    with dve.Fori(0, 2) as i:
                        for t in range(RING):
                            dve.drain()
                            dve.wait_ge(sem["slots_used"], used(name_out, RING * i + (t + 1)))
                            V.scalar_tensor_tensor(res[:, RING * i + t, :], ps[:, 4 + t, :], 0.5,
                                                   res[:, RING * i + t, :], ALU.mult, ALU.add)\
                                .then_inc(sem["down_done"], 1)
                B()

            ffn_dve("ffn1", 0, 0)

            norm_split_dve(dve, "g_mix_0", qk_s, hn_lo)
            B()
            V.tensor_copy(neg_tri_r[:, :], con("neg_tri"))
            V.tensor_copy(neg_ones_r[:, :], con("neg_ones")).then_inc(sem["sums_ready"], 1)

            def softplus(unit, u):
                e, bank = u % 2, 3 * (u % 2)
                dve.wait_ge(sem["log_done"], unit + 1)
                for t in range(TT):
                    b, at = SB_AT[t]
                    V.scalar_tensor_tensor(sp_b[:, e, CUT[t]:CUT[t + 1]], ps[:, bank + b, at:at + T - t * P], 0.0,
                                           lg[:, e, CUT[t]:CUT[t + 1]], ALU.max, ALU.add)
                dve.drain()
                for t in range(TT):
                    d = sp_b[:, e, CUT[t]:CUT[t] + P]
                    V.tensor_tensor(d, d, con("sb_keep"), ALU.mult)
                dve.drain()
                V.tensor_copy(sp_hi[:, e, :], sp_b[:, e, :])
                dve.drain()
                V.tensor_tensor(sp_lo[:, e, :], sp_b[:, e, :], sp_hi[:, e, :].bitcast(F32), ALU.subtract)\
                    .then_inc(sem["sp_ready"], 1)

            softplus(0, 0)
            with dve.Fori(0, SB_PAIRS // 2) as i:
                def store(u):
                    pair, e = u // 2, u % 2
                    dve.wait_ge(sem["pv_done"], 4 * i + (u + 1))
                    V.tensor_copy(hn[64 * e:64 * e + 64, 2 * i + pair, :], ps[64 * e:64 * e + 64, 6 + e, :])\
                        .then_inc(sem["sb_stored"], 1)

                for u in range(4):
                    softplus(4 * i + (u + 1), u + 1)
                    if u > 0:
                        store(u - 1)
                store(3)
            B()
            low_tiles_dve(dve, hn, [(mix_hi, hn_lo)])
            with dve.Fori(0, 2) as i:
                for t in range(RING):
                    dve.wait_ge(sem["slots_used"], used("sb_out", RING * i + (t + 1)))
                    V.tensor_tensor(res[:, RING * i + t, :], ps[:, t, :], res[:, RING * i + t, :], ALU.add)\
                        .then_inc(sem["res_added"], 1)
            B()

            ffn_dve("ffn2", 0, 1)

            norm_split_dve(dve, "g_kv", kt8, hn_lo)
            B()
            for c in range(2):
                for g in range(KV_HEADS):
                    src = kt8[64 * (g % 2):64 * (g % 2) + 64, 2 * c + g // 2, :]
                    V.tensor_copy(x2[0:64, c, g, :], src)
                    V.tensor_copy(x2[64:128, c, g, 0:T - 1], src[:, 1:T])
            dve.drain()
            for c in range(2):
                pos = con("pos_k" if c == 0 else "pos_v")
                for m in range(16):
                    op = V.tensor_scalar(xb[:, c, m, :].rearrange("p (g n) -> p g n", g=KV_HEADS),
                                         x2[:, c, :, 2 * m:2 * m + 16 * (N_CMP - 1) + 1:16],
                                         pos[:, m:m + 1], None, ALU.add)
            op.then_inc(sem["xb_ready"], 1)

            def head_dve(src, xn, t1, t2, gain, rows, cols, cos, sin, dsts, n, root=root):
                dve.wait_ge(sem["hr_root"], n + 1)
                V.reciprocal(rinv[0:rows, 0:cols], root[0:rows, 0:cols])
                dve.drain()
                V.scalar_tensor_tensor(xn[0:rows, 0:cols], src, gain, rinv[0:rows, 0:cols], ALU.mult, ALU.mult)\
                    .then_inc(sem["hr_normed"], 1)
                dve.drain()
                V.tensor_tensor(t1[0:rows, 0:cols], xn[0:rows, 0:cols], cos, ALU.mult)
                dve.wait_ge(sem["hr_rotated"], n + 1)
                V.tensor_tensor(t2[0:rows, 0:cols], ps[0:rows, 1, 0:cols], sin, ALU.mult)
                dve.drain()
                for half, dst in enumerate(dsts):
                    V.tensor_tensor(dst, t1[64 * half:64 * half + 64, 0:cols], t2[64 * half:64 * half + 64, 0:cols],
                                    ALU.add)
                dve.drain()

            dve.wait_ge(sem["cmp_copied"], 1)
            head_dve(kc_raw[0:64, :], hr_xn, hr_t1, hr_t2, con("k_norm")[0:64, 0:1], 64, 124,
                     con("cos_c")[0:64, :], con("sin_c")[0:64, :], [k_c[0:64, :]], 0)
            for m in range(4):
                br, pair = m // 2, m % 2
                head_dve(kt8[:, 4 + m, :], hr_xn, hr_t1, hr_t2, con("k_norm")[:, 1 + br:2 + br], P, T,
                         con("cos"), con("sin"),
                         [k_sw[0:64, 4 * br + 2 * pair + half, :] for half in range(2)], 1 + m)
            B()

            ffn_dve("ffn1", 1, 2)

            norm_split_dve(dve, "g_mix_1", nsa_tmp, hn_lo)
            B()
            for t in range(TT):
                V.tensor_scalar(gts[:, t, 0:16], gts[:, t, 0:16], con("valid")[:, t:t + 1], None, ALU.mult)
            with dve.Fori(0, DT // 2) as i:
                for b in range(2):
                    head_dve(q_t[:, 2 * i + b, :], hr2_xn, hr2_t1, hr2_t2, con("q_norm"), P, T, con("cos"), con("sin"),
                             [q_h[0:64, 4 * i + (2 * b + half), :] for half in range(2)], 2 * i + (b + 5),
                             hr2_root[:, b, :])
            B()
            def maxima(unit, u):
                br, b, bank = u % 3, u % 2, 3 * (u % 2)
                dve.wait_ge(sem["z2_done"], unit + 7)
                if br < 2:
                    for t in range(TT):
                        tb, at = NSA_AT[t]
                        V.tensor_reduce(zraw[:, b, t:t + 1], ps[:, bank + tb, at:at + (t + 1) * P], AX, ALU.max)
                else:
                    V.tensor_reduce(zraw[:, b, :], ps[:, bank + 1, 0:TT * N_CMP].rearrange("p (t n) -> p t n", t=TT),
                                    AX, ALU.max)
                dve.drain()
                V.tensor_scalar(zmax[:, b, :], zraw[:, b, :], -(HD ** -0.5), None, ALU.mult)\
                    .then_inc(sem["max_ready"], 1)

            maxima(0, 0)
            with dve.Fori(0, SB_PAIRS) as p:
                def copy_turned(u):
                    b, bank = u % 2, 3 * (u % 2)
                    rows, cols = (P, T) if u % 3 < 2 else (N_CMP, 2 * P)
                    dve.wait_ge(sem["turned"], 6 * p + (u + 1))
                    V.tensor_copy(prt[0:rows, b, 0:cols], ps[0:rows, bank, 0:cols]).then_inc(sem["first_turned"], 1)

                def combine(u):
                    e, br, b = u // 3, u % 3, u % 2
                    col = (16, 32, 0)[br]
                    dve.wait_ge(sem["attended"], 6 * p + (u + 1))
                    V.reciprocal(psm[:, br, :], psm[:, br, :])
                    dve.drain()
                    V.tensor_tensor(coef[:, b, :], psm[:, br, :], gts_g[:, 2 * p + (col + e), :], ALU.mult)
                    dve.drain()
                    for t in range(TT):
                        o = o_n4[:, t, 2 * p + e, :]
                        src = ps[:, 6 + b, t * HD:(t + 1) * HD]
                        if br == 0:
                            op = V.tensor_scalar(o, src, coef[:, b, t:t + 1], None, ALU.mult)
                        else:
                            op = V.scalar_tensor_tensor(o, src, coef[:, b, t:t + 1], o, ALU.mult, ALU.add)
                    op.then_inc(sem["combined"], 1)
                    dve.drain()

                for u in range(6):
                    maxima(6 * p + (u + 1), u + 1)
                    copy_turned(u)
                    if u > 0:
                        combine(u - 1)
                combine(5)
            B()
            B()
            low_tiles_dve(dve, hn, [(mix_hi, hn_lo)])
            with dve.Fori(0, 2) as i:
                for t in range(RING):
                    dve.wait_ge(sem["slots_used"], used("nsa_out", RING * i + (t + 1)))
                    V.tensor_tensor(res[:, RING * i + t, :], ps[:, t, :], res[:, RING * i + t, :], ALU.add)\
                        .then_inc(sem["res_added"], 1)
            B()
            ffn_dve("ffn2", 1, 3)

        @block.gpsimd
        def _(pool):
            G = nc.gpsimd
            B = lambda: barrier(pool, "pool")
            pool.wait_ge(sem["const_landed"], 16)
            for dst, name in ((ident_1, "ident"), (causal_1, "causal_neg"), (sb_neg_1, "sb_neg"), (neg_c_1, "neg_c")):
                G.tensor_copy(dst, con(name))
            def lows(*names):
                lows_pool(pool, names)
                B()

            lows("even_in")
            lows("even_out")
            B()
            lows("odd_qk", "odd_r", "odd_v")
            w_gate = con("w_gate_lr").rearrange("p (h d c) -> p h d c", h=GLA_HEADS, d=2)
            bias = con("gla_bias").rearrange("p (h d) -> p h d", d=2)
            v4 = v_o.rearrange("p t (h e) -> p t h e", h=GLA_HEADS)
            def gla_inputs(head):
                G.tensor_copy(wz[0:32, :, :], w_gate[0:32, head, :, :])
                G.tensor_copy(bz, bias[:, head, :])
                pool.drain().then_inc(sem["gate_inputs"], 1)

            gla_inputs(0)
            with pool.Fori(0, GLA_HEADS // 2) as i:
                for b in range(2):
                    pool.wait_ge(sem["gate_log"], 2 * i + (b + 1))
                    gla_inputs(2 * i + 1 if b == 0 else (i + 1) % 2 * 2)
                    pool.wait_ge(sem["o_done"], 2 * i + (b + 1))
                    G.tensor_copy(vh[:, :, :], v4[:, :, 2 * i + b, :])
                    pool.drain().then_inc(sem["v_ready"], 1)
            B()
            lows("odd_out")
            B()
            lows(*(name for name, _, _ in ffn_stream("ffn1", 0)))
            lows("sb_q", "sb_k", "sb_v")
            v3 = v_s.rearrange("p t (g d) -> p t g d", d=P)
            with pool.Fori(0, SB_PAIRS // 2) as i:
                for pair in range(2):
                    pool.wait_ge(sem["z_done"], 4 * i + (2 * pair + 2))
                    G.tensor_copy(q_st[:, pair, :], qk_s[:, 2 * i + pair, :])
                    G.tensor_copy(k_st_s[:, pair, :], qk_s[:, 2 * i + (pair + 8), :])
                    pool.drain().then_inc(sem["sb_copies"], 1)
                    pool.wait_ge(sem["sb_stored"], 4 * i + (2 * pair + 1))
                    G.tensor_copy(v_st[:, pair, :, :], v3[:, :, 2 * i + pair, :])
                    pool.drain().then_inc(sem["sb_values"], 1)
            pool.wait_ge(sem["sb_stored"], 2 * SB_PAIRS + 1)
            pool.sem_inc(sem["sb_copies"], 1)
            B()
            lows("sb_out")
            lows(*(name for name, _, _ in ffn_stream("ffn2", 0)))
            lows("kv_t", "kv_v")
            B()
            lows(*(name for name, _, _ in ffn_stream("ffn1", 1)))
            lows("nsa_q")
            B()
            with pool.Fori(0, SB_PAIRS) as p:
                for e in range(2):
                    pool.wait_ge(sem["z2_done"], 6 * p + (3 * e + 3))
                    G.tensor_copy(q_s2[0:64, e, :], q_h[0:64, 2 * p + e, :])
                    pool.drain().then_inc(sem["q_static"], 1)
            pool.wait_ge(sem["z2_done"], 6 * SB_PAIRS + 3)
            G.tensor_copy(q_s2[0:64, 0, :], q_h[0:64, 0, :])
            pool.drain().then_inc(sem["q_static"], 1)
            B()
            B()
            lows("nsa_out")
            lows(*(name for name, _, _ in ffn_stream("ffn2", 1)))



        assert set(phase["n"].values()) == {phase_total}, phase["n"]


def by_tiles(w):
    k, m = w.shape
    return w.reshape(k // P, P, m // P, P).transpose(2, 1, 0, 3).reshape(m // P, P, k)


def in_parts(w, parts):
    k, m = w.shape
    return w.reshape(parts, k // P // parts, P, m // P, P).transpose(3, 0, 2, 1, 4).reshape(m // P * parts, P, k // parts)


def by_columns(w):
    k, m = w.shape
    return w.reshape(4, 2, P, m // 512, 512).transpose(3, 0, 2, 1, 4).reshape(m // 128, P, 1024)


def col(v):
    return v.reshape(-1, P).T


def tables():
    f = np.float32
    t = {}
    a, b = np.arange(P)[:, None], np.arange(P)[None, :]
    t["ident"] = (a == b).astype(f)
    t["ones"] = np.ones((P, P), f)
    t["halves"] = (a // 64 == b // 64).astype(f)
    rot = np.zeros((P, P), f)
    for base in (0, 64):
        for d in range(8):
            rot[base + d + 8, base + d] = -1.0
            rot[base + d, base + d + 8] = 1.0
    t["rot"] = rot
    t["neg_tri"] = -(a >= b).astype(f)
    t["neg_ones"] = -np.ones((P, P), f)
    t["sb_neg"] = np.where(a >= b, NEG, 0.0).astype(f)
    t["sb_keep"] = (a < b).astype(f)
    t["causal_neg"] = np.where(b > a, NEG, 0.0).astype(f)
    same = a // GLA_CHUNK == b // GLA_CHUNK
    t["gla_keep"] = np.concatenate([np.tile((same & (a <= b)).astype(f), (1, TT)),
                                    np.tile((same & (a >= b)).astype(f), (1, TT))], 1)
    tok = np.arange(T)
    keep = np.stack([tok % GLA_CHUNK != 0, tok % GLA_CHUNK != GLA_CHUNK - 1]).astype(f)
    t["chunk_keep"] = np.broadcast_to(keep.reshape(1, 2 * T), (P, 2 * T))
    inv_freq = np.power(f(500000.0), -np.arange(0, 16, 2, dtype=f) / f(16)).astype(f)

    def rope(positions):
        ang = positions.astype(f)[None, :] * inv_freq[:, None]
        n = len(positions)
        c, s = np.ones((64, n), f), np.zeros((64, n), f)
        c[0:8] = c[8:16] = np.cos(ang)
        s[0:8] = s[8:16] = np.sin(ang)
        return np.concatenate([c, c]), np.concatenate([s, s])

    t["cos"], t["sin"] = rope(tok)
    ends = np.arange(N_CMP) * 16 + 31
    c, s = rope(ends)
    t["cos_c"], t["sin_c"] = np.tile(c, (1, KV_HEADS)), np.tile(s, (1, KV_HEADS))
    query = np.arange(TT)[None, :, None] * P + np.arange(P)[:, None, None]
    t["neg_c"] = np.where(ends[None, None, :] <= query, 0.0, NEG).astype(f).reshape(P, TT * N_CMP)
    t["valid"] = (query[:, :, 0] >= 31).astype(f)
    t["eps"] = np.full((P, 1), EPS, f)
    return t


def kernel(**inputs):
    import concourse.bacc as bacc
    from concourse.bass_utils import run_bass_kernel_spmd

    a = {k: np.asarray(v) for k, v in inputs.items()}
    c = tables()
    for name, v in (("even_pre", a["even_norm_pre"][0]), ("even_post", a["even_norm_post"][0]),
                    ("odd_pre", a["odd_norm_pre"][0]), ("odd_post", a["odd_norm_post"][0]),
                    ("ffn1_0", a["ffn1_norm_2"][0]), ("ffn1_1", a["ffn1_norm_2"][1]),
                    ("mix_0", a["mix_norm_2"][0]), ("mix_1", a["mix_norm_2"][1]),
                    ("ffn2_0", a["ffn2_norm_2"][0]), ("ffn2_1", a["ffn2_norm_2"][1]), ("kv", a["kv_norm_2"])):
        c["g_" + name] = col(v)
    c["lam"] = a["rg_lambda"][0].reshape(2, RG_HEADS, P).transpose(2, 1, 0).reshape(P, 16)
    c["gla_bias"] = a["gla_b_gate"][0].reshape(2, GLA_HEADS, P).transpose(2, 1, 0).reshape(P, 8)
    c["gla_g"] = col(a["gla_norm_g"][0])
    c["q_norm"] = np.tile(a["nsa_q_norm_2"][0], 2).reshape(P, 1)
    c["k_norm"] = np.tile(a["nsa_k_norm_2"].T, (2, 1))
    c["pos_k"] = a["cmp_pos_k_2"].reshape(16, P).T
    c["pos_v"] = a["cmp_pos_v_2"].reshape(16, P).T
    w_odd = a["odd_w_in"][0]
    c["w_lr"] = w_odd[:, 3072:3104].reshape(DT, P, 32).transpose(1, 0, 2).reshape(P, 256)
    gate_lr = np.zeros((P, GLA_HEADS, 2, P), np.float32)
    for d in range(2):
        gate_lr[d * GLA_RANK:(d + 1) * GLA_RANK, :, d, :] = a["gla_w_gate_lr"][0, d].reshape(GLA_RANK, GLA_HEADS, P)
    c["w_gate_lr"] = gate_lr.reshape(P, -1)
    c["w2_k"] = a["cmp_k_w2_2"].reshape(2, P, HD).transpose(1, 0, 2).reshape(P, 128)
    c["w2_v"] = a["cmp_v_w2_2"].reshape(2, P, HD).transpose(1, 0, 2).reshape(P, 128)
    w_nsa = a["nsa_w_in_2"][0]
    c["w_gates"] = w_nsa[:, D:].reshape(DT, P, 48).transpose(1, 0, 2).reshape(P, 384)
    consts = np.concatenate([np.asarray(c[name], np.float32).reshape(P, n) for name, n in CONSTS], 1)

    gates = np.zeros((RG_HEADS, P, GATE_COLS), np.float32)
    gates[:, :, 0:4 * P] = a["rg_gate_w"][0].reshape(4, RG_HEADS, P, P).transpose(1, 2, 0, 3).reshape(RG_HEADS, P, 4 * P)
    gates[:, :, 4 * P:4 * P + 4] = a["rg_gate_b"][0].reshape(4, RG_HEADS, P).transpose(1, 2, 0)
    gates[:, :, 4 * P + 4:4 * P + 8] = a["rg_conv_w"][0].reshape(4, RG_HEADS, P).transpose(1, 2, 0)
    gates[:, :, 4 * P + 8] = a["rg_conv_b"][0].reshape(RG_HEADS, P)
    gates[:, :, 4 * P + 9:4 * P + 12] = a["sc_conv_w"][0].reshape(3, RG_HEADS, P).transpose(1, 2, 0)

    w = {}
    ev = by_tiles(a["even_w_in"][0]).reshape(6, DT, P, D)
    w["even_in"] = ev[[0, 2, 4, 3, 5, 1]].transpose(1, 0, 2, 3).reshape(48, P, D)
    w["even_out"] = in_parts(a["even_w_out"][0], 2)
    w["odd_qk"], w["odd_r"] = by_tiles(w_odd[:, 0:1024]), by_tiles(w_odd[:, 2048:3072])
    w["odd_v"] = by_columns(w_odd[:, 1024:2048])
    w["odd_out"] = by_tiles(a["odd_w_out"][0])
    for which in ("ffn1", "ffn2"):
        for layer in range(2):
            both = by_tiles(a[f"{which}_w_in_2"][layer]).reshape(2, FT, P, D).transpose(1, 0, 2, 3)
            down = a[f"{which}_w_out_2"][layer]
            for half, n in enumerate(HALVES):
                tiles = slice(HALVES[0] * half, HALVES[0] * half + n)
                w[f"{which}_in_{layer}_{half}"] = both[tiles].reshape(2 * n, P, D)
                w[f"{which}_out_{layer}_{half}"] = by_tiles(down[tiles.start * P:tiles.stop * P])
    qkv = a["sb_w_qkv_2"][0]
    w["sb_q"], w["sb_k"], w["sb_v"] = by_tiles(qkv[:, 0:1024]), by_tiles(qkv[:, 1024:2048]), by_columns(qkv[:, 2048:3072])
    w["sb_out"] = by_tiles(a["sb_w_out_2"][0])
    kv = a["nsa_w_kv_2"]
    part = [kv[:, 256 * i:256 * (i + 1)] for i in range(6)]
    w["kv_t"] = by_tiles(np.concatenate([part[0], part[1], part[2], part[4]], 1))
    w["kv_v"] = by_columns(np.concatenate([part[3], part[5]], 1))
    w["cmp_w1"] = np.concatenate([a[n].reshape(4, 4, P, 2, P).transpose(0, 2, 1, 3, 4).reshape(4, P, 1024)
                                  for n in ("cmp_k_w1_2", "cmp_v_w1_2")], 0)
    w["nsa_q"] = by_tiles(w_nsa[:, 0:D])
    w["nsa_out"] = by_tiles(a["nsa_w_out_2"][0])

    arrays = {"x": a["x"][0].T.reshape(DT, P, T).transpose(1, 0, 2), "consts": consts, "gates": gates}
    arrays.update(w)
    arrays = {k: np.ascontiguousarray(v) for k, v in arrays.items()}
    nc = bacc.Bacc("TRN2", target_bir_lowering=False, num_devices=1)
    aps = {k: nc.dram_tensor(f"in_{k}", v.shape, F32, kind="ExternalInput").ap() for k, v in arrays.items()}
    out = nc.dram_tensor("out_y", (P, DT, T), F32, kind="ExternalOutput").ap()
    build(nc, aps["x"], aps["consts"], aps["gates"], {name: aps[name] for name, _, _ in STREAM}, out)
    got = run_bass_kernel_spmd(nc, [{f"in_{k}": v for k, v in arrays.items()}], core_ids=[0])
    y = got.results[0]["out_y"]
    return np.ascontiguousarray(y.transpose(2, 1, 0).reshape(1, T, D))
```
